# Optimizing a Trainium2 kernel written in Bass

```python
import jax, jax.numpy as jnp
from jax import lax
import numpy as np

D_MODEL = 1024
BATCH = 1
SEQ = 256
DEPTH = 1

D_MIX = D_MODEL
HEAD_DIM = 64
MLSTM_HEADS = (D_MIX // 2) // HEAD_DIM
MOBA_HEADS = (D_MIX // 2) // HEAD_DIM
MLSTM_WIDTH = MLSTM_HEADS * HEAD_DIM
MOBA_WIDTH = MOBA_HEADS * HEAD_DIM
MLSTM_CHUNK = 128
CONV_WIDTH = 4
MOBA_BLOCK = 256
MOBA_TOPK = 3
MOBA_Q_CHUNK = 64
N_EXPERTS = 32
TOP_K = 4
D_FF = D_MODEL
SWIGLU_LIMIT = 7.0
SWIGLU_ALPHA = 1.702
PLE_DIM = 256
RMS_EPS = 1e-6
PROJ_COLS = 4 * MLSTM_WIDTH + 2 * MLSTM_HEADS + 3 * MOBA_WIDTH

kernel_name = "hymba_mlstm_moba_moe_block"

def rmsnorm(x, g):
    xf = x.astype(jnp.float32)
    y = xf * lax.rsqrt(jnp.mean(xf * xf, axis=-1, keepdims=True) + RMS_EPS)
    return (y * g.astype(jnp.float32)).astype(x.dtype)

def alibi_slopes(n_heads):
    return jnp.exp2(-8.0 * jnp.arange(1, n_heads + 1, dtype=jnp.float32) / n_heads)

def causal_conv_silu(u, w, b):
    K = w.shape[0]
    S = u.shape[1]
    up = jnp.pad(u, ((0, 0), (K - 1, 0), (0, 0)))
    y = b + up[:, 0:S] * w[0]
    for j in range(1, K):
        y = y + up[:, j:j + S] * w[j]
    return jax.nn.silu(y)

def mlstm_chunkwise(q, k, v, i_pre, f_pre):
    B, H, S, Dh = q.shape
    L = MLSTM_CHUNK
    NC = S // L
    lf = jax.nn.log_sigmoid(f_pre.astype(jnp.float32))

    def to_chunks(a):
        a = a.astype(jnp.float32)
        return jnp.moveaxis(a.reshape(a.shape[:2] + (NC, L) + a.shape[3:]), 2, 0)

    xs = (to_chunks(q), to_chunks(k), to_chunks(v), to_chunks(i_pre), to_chunks(lf))
    causal = jnp.tril(jnp.ones((L, L), dtype=bool))

    def step(carry, inp):
        C, n, m = carry
        q_, k_, v_, i_, f_ = inp
        b = jnp.cumsum(f_, axis=-1)
        logD = b[..., :, None] - b[..., None, :] + i_[..., None, :]
        logD = jnp.where(causal, logD, -jnp.inf)
        inter = b + m[..., None]
        m_t = jnp.maximum(inter, jnp.max(logD, axis=-1))
        Dm = jnp.exp(logD - m_t[..., None])
        sc_inter = jnp.exp(inter - m_t)
        s = jnp.einsum('bhtd,bhsd->bhts', q_, k_) * Dm
        num = jnp.einsum('bhts,bhsd->bhtd', s, v_) + sc_inter[..., None] * jnp.einsum('bhvk,bhtk->bhtv', C, q_)
        den = jnp.sum(s, axis=-1) + sc_inter * jnp.einsum('bhk,bhtk->bht', n, q_)
        h = num / jnp.maximum(jnp.abs(den), jnp.exp(-m_t))[..., None]
        bL = b[..., -1]
        logw = bL[..., None] - b + i_
        m_new = jnp.maximum(bL + m, jnp.max(logw, axis=-1))
        w = jnp.exp(logw - m_new[..., None])
        decay = jnp.exp(bL + m - m_new)
        C_new = decay[..., None, None] * C + jnp.einsum('bhs,bhsv,bhsk->bhvk', w, v_, k_)
        n_new = decay[..., None] * n + jnp.einsum('bhs,bhsk->bhk', w, k_)
        return (C_new, n_new, m_new), h

    init = (jnp.zeros((B, H, Dh, Dh), jnp.float32), jnp.zeros((B, H, Dh), jnp.float32),
            jnp.zeros((B, H), jnp.float32))
    _, hs = lax.scan(step, init, xs)
    return jnp.moveaxis(hs, 0, 2).reshape(B, H, S, Dh)

def moba_attention(q, k, v):
    B, H, S, Dh = q.shape
    BS = MOBA_BLOCK
    Qc = MOBA_Q_CHUNK
    S_pad = -(-S // BS) * BS
    q = q.astype(jnp.float32)
    pad = ((0, 0), (0, 0), (0, S_pad - S), (0, 0))
    k = jnp.pad(k.astype(jnp.float32), pad)
    v = jnp.pad(v.astype(jnp.float32), pad)
    NB = S_pad // BS
    n_sel = min(MOBA_TOPK, NB)
    kb = k.reshape(B, H, NB, BS, Dh)
    vb = v.reshape(B, H, NB, BS, Dh)
    kmean = jnp.mean(kb, axis=3)
    slopes = alibi_slopes(H)
    blk_ids = jnp.arange(NB)
    in_blk = jnp.arange(BS)
    gather = jax.vmap(jax.vmap(lambda blocks, idx: blocks[idx]))

    def one_chunk(c):
        t0 = c * Qc
        qc = lax.dynamic_slice_in_dim(q, t0, Qc, axis=2)
        pos_q = t0 + jnp.arange(Qc)
        own = t0 // BS
        gate = jnp.einsum('bhqd,bhnd->bhqn', qc, kmean)
        gate = jnp.where(blk_ids < own, gate, -jnp.inf)
        _, sel = lax.top_k(gate, n_sel)
        sel_valid = sel < own
        ks = gather(kb, sel)
        vs = gather(vb, sel)
        s_sel = jnp.einsum('bhqd,bhqjkd->bhqjk', qc, ks)
        pos_sel = sel[..., None] * BS + in_blk
        dist_sel = (pos_q[:, None, None] - pos_sel).astype(jnp.float32)
        s_sel = s_sel - slopes[:, None, None, None] * dist_sel
        s_sel = jnp.where(sel_valid[..., None], s_sel, -jnp.inf)
        k_own = lax.dynamic_index_in_dim(kb, own, axis=2, keepdims=False)
        v_own = lax.dynamic_index_in_dim(vb, own, axis=2, keepdims=False)
        s_own = jnp.einsum('bhqd,bhkd->bhqk', qc, k_own)
        dist_own = pos_q[:, None] - (own * BS + in_blk)[None, :]
        s_own = s_own - slopes[:, None, None] * dist_own.astype(jnp.float32)
        s_own = jnp.where(dist_own >= 0, s_own, -jnp.inf)
        scores = jnp.concatenate([s_sel.reshape(B, H, Qc, n_sel * BS), s_own], axis=-1)
        probs = jax.nn.softmax(scores, axis=-1)
        p_sel = probs[..., :n_sel * BS].reshape(B, H, Qc, n_sel, BS)
        p_own = probs[..., n_sel * BS:]
        return (jnp.einsum('bhqjk,bhqjkd->bhqd', p_sel, vs)
                + jnp.einsum('bhqk,bhkd->bhqd', p_own, v_own))

    outs = lax.map(one_chunk, jnp.arange(S // Qc))
    return jnp.moveaxis(outs, 0, 2).reshape(B, H, S, Dh)

def moe_ffn(h, w_router, b_router, w_gu, b_gu, w_dn, b_dn):
    B, S, D = h.shape
    t = h.reshape(B * S, D)
    logits = (t @ w_router + b_router).astype(jnp.float32)
    top_vals, top_idx = lax.top_k(logits, TOP_K)
    wts = jax.nn.softmax(top_vals, axis=-1)
    gates = jnp.sum(jax.nn.one_hot(top_idx, N_EXPERTS, dtype=jnp.float32) * wts[..., None], axis=1)
    y = jnp.zeros((B * S, D), jnp.float32)
    for e in range(N_EXPERTS):
        hu = t @ w_gu[e] + b_gu[e]
        glu = jnp.minimum(hu[:, :D_FF], SWIGLU_LIMIT)
        lin = jnp.clip(hu[:, D_FF:], -SWIGLU_LIMIT, SWIGLU_LIMIT)
        act = glu * jax.nn.sigmoid(SWIGLU_ALPHA * glu) * (lin + 1.0)
        y = y + gates[:, e:e + 1] * (act @ w_dn[e] + b_dn[e])
    return y.reshape(B, S, D)

def setup_inputs(seed: int = 0) -> dict:
    key = jax.random.key(seed)
    ks = jax.random.split(key, 24)
    L = DEPTH

    def nrm(k, shape, scale):
        return jax.random.normal(k, shape, jnp.float32) * scale

    return {
        "x": nrm(ks[0], (BATCH, SEQ, D_MODEL), 1.0),
        "p": nrm(ks[1], (DEPTH, BATCH, SEQ, PLE_DIM), 1.0),
        "mix_norm_g": 1.0 + nrm(ks[2], (L, D_MODEL), 0.02),
        "w_in": nrm(ks[3], (L, D_MODEL, PROJ_COLS), D_MODEL ** -0.5),
        "conv_w": nrm(ks[4], (L, CONV_WIDTH, 2 * MLSTM_WIDTH), CONV_WIDTH ** -0.5),
        "conv_b": nrm(ks[5], (L, 2 * MLSTM_WIDTH), 0.02),
        "igate_b": nrm(ks[6], (L, MLSTM_HEADS), 0.1),
        "fgate_b": jnp.linspace(3.0, 6.0, MLSTM_HEADS, dtype=jnp.float32) + nrm(ks[7], (L, MLSTM_HEADS), 0.1),
        "mlstm_head_g": 1.0 + nrm(ks[8], (L, MLSTM_HEADS, HEAD_DIM), 0.02),
        "q_norm_g": 1.0 + nrm(ks[9], (L, HEAD_DIM), 0.02),
        "k_norm_g": 1.0 + nrm(ks[10], (L, HEAD_DIM), 0.02),
        "w_out": nrm(ks[11], (L, D_MIX, D_MODEL), D_MIX ** -0.5),
        "ffn_norm_g": 1.0 + nrm(ks[12], (L, D_MODEL), 0.02),
        "w_router": nrm(ks[13], (L, D_MODEL, N_EXPERTS), D_MODEL ** -0.5),
        "b_router": nrm(ks[14], (L, N_EXPERTS), 0.01),
        "w_gate_up": nrm(ks[15], (L, N_EXPERTS, D_MODEL, 2 * D_FF), D_MODEL ** -0.5),
        "b_gate_up": nrm(ks[16], (L, N_EXPERTS, 2 * D_FF), 0.02),
        "w_down": nrm(ks[17], (L, N_EXPERTS, D_FF, D_MODEL), D_FF ** -0.5),
        "b_down": nrm(ks[18], (L, N_EXPERTS, D_MODEL), 0.02),
        "ple_norm_g": 1.0 + nrm(ks[19], (L, D_MODEL), 0.02),
        "w_ple_gate": nrm(ks[20], (L, D_MODEL, D_MODEL), D_MODEL ** -0.5),
        "w_ple_proj": nrm(ks[21], (L, PLE_DIM, D_MODEL), PLE_DIM ** -0.5),
    }

def reference(x, p, mix_norm_g, w_in, conv_w, conv_b, igate_b, fgate_b, mlstm_head_g,
              q_norm_g, k_norm_g, w_out, ffn_norm_g, w_router, b_router, w_gate_up,
              b_gate_up, w_down, b_down, ple_norm_g, w_ple_gate, w_ple_proj):
    B, S, _ = x.shape
    Wm, Hm, Wb, Hb = MLSTM_WIDTH, MLSTM_HEADS, MOBA_WIDTH, MOBA_HEADS
    splits = [2 * Wm, 3 * Wm, 4 * Wm, 4 * Wm + Hm, 4 * Wm + 2 * Hm,
              4 * Wm + 2 * Hm + Wb, 4 * Wm + 2 * Hm + 2 * Wb]

    def heads(a, n):
        return a.reshape(B, S, n, HEAD_DIM).transpose(0, 2, 1, 3)

    scale = HEAD_DIM ** -0.5
    for l in range(DEPTH):
        h = rmsnorm(x, mix_norm_g[l])
        u = h @ w_in[l]
        ml_qk, ml_v, ml_o, ml_i, ml_f, mb_q, mb_k, mb_v = jnp.split(u, splits, axis=-1)

        ml_qk = causal_conv_silu(ml_qk, conv_w[l], conv_b[l])
        q_m = heads(ml_qk[..., :Wm], Hm) * scale
        k_m = heads(ml_qk[..., Wm:], Hm)
        v_m = heads(ml_v, Hm)
        i_pre = (ml_i + igate_b[l]).transpose(0, 2, 1)
        f_pre = (ml_f + fgate_b[l]).transpose(0, 2, 1)
        h_m = mlstm_chunkwise(q_m, k_m, v_m, i_pre, f_pre)
        h_m = rmsnorm(h_m, mlstm_head_g[l][:, None, :])
        h_m = h_m.transpose(0, 2, 1, 3).reshape(B, S, Wm) * jax.nn.sigmoid(ml_o.astype(jnp.float32))

        q_b = rmsnorm(heads(mb_q, Hb), q_norm_g[l]) * scale
        k_b = rmsnorm(heads(mb_k, Hb), k_norm_g[l])
        v_b = heads(mb_v, Hb)
        h_b = moba_attention(q_b, k_b, v_b).transpose(0, 2, 1, 3).reshape(B, S, Wb)

        mix = jnp.concatenate([h_m, h_b], axis=-1).astype(x.dtype) @ w_out[l]
        x = x + mix.astype(x.dtype)

        y = moe_ffn(rmsnorm(x, ffn_norm_g[l]), w_router[l], b_router[l], w_gate_up[l],
                    b_gate_up[l], w_down[l], b_down[l])
        x = x + y.astype(x.dtype)

        g = jax.nn.sigmoid((rmsnorm(x, ple_norm_g[l]) @ w_ple_gate[l]).astype(jnp.float32))
        x = x + (g * (p[l] @ w_ple_proj[l]).astype(jnp.float32)).astype(x.dtype)
    return x


_drawn_inputs = setup_inputs


def setup_inputs(seed=0):
    import zlib

    import numpy as np

    out = dict(_drawn_inputs(seed))
    spreads = {}
    factors = {'igate_b': 64.0,
     'q_norm_g': 4.822,
     'b_gate_up': 5.928,
     'b_down': 6.833,
     'ple_norm_g': 46.166}
    for name, (base, spread) in spreads.items():
        noise = np.random.default_rng([zlib.crc32(name.encode()), seed]).standard_normal(out[name].shape)
        drawn = base * np.exp(spread * noise) if base else spread * noise
        out[name] = __import__('jax').numpy.asarray(drawn.astype(out[name].dtype))
    for name, factor in factors.items():
        out[name] = (out[name] * factor).astype(out[name].dtype)
    return out
```

```python
from contextlib import ExitStack

import concourse.bass as bass
from concourse import mybir

F32 = mybir.dt.float32
I32 = mybir.dt.int32
U32 = mybir.dt.uint32
ALU = mybir.AluOpType
ACT = mybir.ActivationFunctionType
AX = mybir.AxisListType

P = 128
EPS = 1e-6
LIMIT = 7.0
ALPHA = 1.702
TOP_K = 4
MASKED = -1.0e30
RING = 6
SLOTS = 64


def hybrid_layer(nc, x, p, mix_norm_g, w_in, conv_w, conv_b, igate_b, fgate_b, mlstm_head_g, q_norm_g,
                 k_norm_g, w_out, ffn_norm_g, w_router, b_router, w_gate_up, b_gate_up, w_down, b_down,
                 ple_norm_g, w_ple_gate, w_ple_proj, out):
    S, D = x.shape[1:]
    H, DH = mlstm_head_g.shape[1:]
    E = w_router.shape[2]
    PLE = p.shape[3]
    K = D // P
    TT = S // P
    W = H * DH
    CONV = conv_w.shape[1]
    PAIRS = E // 2
    NB = 512
    HALVES = D // NB
    IG = 4 * W
    SECTIONS = [2 * W, 4 * W + 2 * H, 4 * W + 2 * H + W, 4 * W + 2 * H + 2 * W, 3 * W]
    SEC_V, SEC_Q, SEC_K, SEC_MV, SEC_O = range(5)
    FIRST_SECTION = 2
    CHUNK_PLE, CHUNK_WO = 7, 8
    MOE0 = 10
    LATE = 16 * 9
    ROUTE_MASK, ROUTE_GATES = 10, 16
    GATE_STEPS = 10
    PER_PAIR = K + K // 2
    TRI = P + S
    assert S == 2 * P and D == 2 * NB and W == NB and 2 * DH == P and PLE == 2 * P and E == 32
    assert PER_PAIR == 2 * RING

    ctx = ExitStack()
    with ctx:
        def sb(name, shape, dt=F32):
            return ctx.enter_context(nc.sbuf_tensor(name, shape, dt))

        def sem(name):
            return ctx.enter_context(nc.semaphore(name))

        hu = ctx.enter_context(nc.psum_tensor("hu", [P, 4, NB], F32))
        po = ctx.enter_context(nc.psum_tensor("po", [P, 2, NB], F32))
        aux = ctx.enter_context(nc.psum_tensor("aux", [P, 2, NB], F32))

        ring = sb("ring", [P, RING, 4096])
        ident = sb("ident", [P, P])
        tri = sb("tri", [P, P])
        before = sb("before", [P, P])
        ones = sb("ones", [P, P])
        dist = sb("dist", [P, TRI])
        sel_head = sb("sel_head", [H, H, P])
        iota_e = sb("iota_e", [P, E])
        iota_s = sb("iota_s", [P, SLOTS])
        cols = sb("cols", [P, K, 9])
        g_ffn = sb("g_ffn", [P, D])
        g_head = sb("g_head", [P, W])
        brb = sb("brb", [P, E])
        ig_bias = sb("ig_bias", [H, 1])
        fg_bias = sb("fg_bias", [H, 1])
        w_if = sb("w_if", [P, K, 2 * H])
        w_r = sb("w_r", [P, K, E])
        bgu = sb("bgu", [P, NB])
        xt = sb("xt", [P, TT, D])
        hT = sb("hT", [P, K, S])
        mixT = sb("mixT", [P, K, S])
        big1 = sb("big1", [P, TT * D])
        big2 = sb("big2", [P, K * S])
        big3 = sb("big3", [P, K * S])
        pt_in = sb("pt_in", [P, TT, PLE])
        pple = sb("pple", [P, TT, D])
        attn = sb("attn", [P, 2 * TT * H * (DH + 1) + 2 * TT * W])
        arow = sb("arow", [H, S])
        mrow = sb("mrow", [H, S])
        negm = sb("negm", [H, S])
        negmt = sb("negmt", [H, S])
        zrow = sb("zrow", [H, S])
        acol = sb("acol", [P, TT, H])
        emc = sb("emc", [P, TT, H])
        expo = sb("expo", [P, 2, TRI])
        dmat = sb("dmat", [P, 2, TRI])
        smat = sb("smat", [P, 2, TRI])
        stat = sb("stat", [P, 64])
        small = sb("small", [P, 256])
        negmax = sb("negmax", [P, 2, 2])
        psum_ = sb("psum_", [P, 2, 2])
        lg = sb("lg", [P, TT, E])
        top = sb("top", [P, TT, 8])
        topi = sb("topi", [P, TT, 8], U32)
        topf = sb("topf", [P, TT, 8])
        mask = sb("mask", [P, TT, E])
        gates = sb("gates", [P, TT, E])
        posm = sb("posm", [P, TT, E + 2])
        cnt = sb("cnt", [P, 8])
        npass_i = sb("npass_i", [1, 1], I32)

        VX = TT * H * (DH + 1)
        vx = attn[:, 0:VX].rearrange("p (t h d) -> p t h d", t=TT, h=H)
        num = attn[:, VX:2 * VX].rearrange("p (t h d) -> p t h d", t=TT, h=H)
        vb = attn[:, 2 * VX:2 * VX + TT * W].rearrange("p (t n) -> p t n", t=TT)
        og = attn[:, 2 * VX + TT * W:2 * VX + 2 * TT * W].rearrange("p (t n) -> p t n", t=TT)
        sel_expert = attn[:, 0:E * SLOTS].rearrange("p (e s) -> p e s", e=E)
        xg = attn[:, 2 * VX:2 * VX + K * P].rearrange("p (k s) -> p k s", k=K)
        rows = big3[0:9, 0:D]
        fpre, fneg, fln, blog = (big3[0:H, D + i * S:D + (i + 1) * S] for i in range(4))
        pT = big2[:, 0:PLE // P * S].rearrange("p (k s) -> p k s", s=S)
        gT = big2[0:E, 2 * S:3 * S]
        eq = big2[:, 3 * S:4 * S].rearrange("p (t e k) -> p t e k", t=TT, e=E)
        bdn = big2[0:E, D:2 * D]
        sel = dmat[:, 0, 0:P]
        onehot, ghot = (expo[:].rearrange("p a b -> p (a b)")[:, i * S:(i + 1) * S]
                        .rearrange("p (t e s) -> p t e s", t=TT, e=2) for i in range(2))
        ghotT = expo[:].rearrange("p a b -> p (a b)")[:, 2 * S:3 * S]
        xs = big1[:].rearrange("p (t d) -> p t d", t=TT)
        h2 = xs
        qkT = big2[:].rearrange("p (k s) -> p k s", k=K)
        bqT = big3[:].rearrange("p (k s) -> p k s", k=K)
        hm = xs
        normed = mixT[:].rearrange("p k s -> p (k s)").rearrange("p (i n) -> p i n", n=NB)
        glu = qkT[:].rearrange("p k s -> p (k s)")[:, 0:D]
        lin = qkT[:].rearrange("p k s -> p (k s)")[:, D:2 * D]
        sig = bqT[:].rearrange("p k s -> p (k s)")[:, 0:D]
        act_s = bqT[:].rearrange("p k s -> p (k s)")[:, D:2 * D]
        lin2 = big2[:].rearrange("p (t d) -> p t d", t=TT)
        actT = mixT[:].rearrange("p k s -> p (k s)")[:, 0:D].rearrange("p (k s) -> p k s", k=K)
        out_s = mixT[:].rearrange("p k s -> p (k s)")[:, D:2 * D]

        const_ready = sem("const_ready")
        zero_ready = sem("zero_ready")
        x_loaded = sem("x_loaded")
        rows_loaded = sem("rows_loaded")
        small_loaded = sem("small_loaded")
        late_loaded = sem("late_loaded")
        bdn_loaded = sem("bdn_loaded")
        sel_built = sem("sel_built")
        ring_full = [sem(f"ring_full{i}") for i in range(RING)]
        chunk_done = sem("chunk_done")
        cols_ps = sem("cols_ps")
        cols_ready = sem("cols_ready")
        ss_ready = sem("ss_ready")
        rstd_step = sem("rstd_step")
        root_ready = sem("root_ready")
        xs_ready = sem("xs_ready")
        xT_ps = sem("xT_ps")
        hT_act = sem("hT_act")
        hT_dve = sem("hT_dve")
        gate_ps = sem("gate_ps")
        gate_step = sem("gate_step")
        gate_act = sem("gate_act")
        gcol_ps = sem("gcol_ps")
        acol_ready = sem("acol_ready")
        emc_ready = sem("emc_ready")
        qk_ps = sem("qk_ps")
        conv_step = sem("conv_step")
        qk_ready = sem("qk_ready")
        half_ps = sem("half_ps")
        v_ready = sem("v_ready")
        sq_ready = sem("sq_ready")
        nstat = sem("nstat")
        nroot = sem("nroot")
        normed_ready = sem("normed_ready")
        normT_ps = sem("normT_ps")
        bqT_ready = sem("bqT_ready")
        vb_ready = sem("vb_ready")
        og_ready = sem("og_ready")
        ogg_ready = sem("ogg_ready")
        mscore_ps = sem("mscore_ps")
        expo_ready = sem("expo_ready")
        dmat_ready = sem("dmat_ready")
        dmask_ready = sem("dmask_ready")
        smat_ready = sem("smat_ready")
        num_ps = sem("num_ps")
        num_ready = sem("num_ready")
        post_step = sem("post_step")
        post_act = sem("post_act")
        post_sq = sem("post_sq")
        hm_ready = sem("hm_ready")
        hmT_ps = sem("hmT_ps")
        hmT_ready = sem("hmT_ready")
        bscore_ps = sem("bscore_ps")
        bias_ready = sem("bias_ready")
        bmax_ready = sem("bmax_ready")
        prob_ready = sem("prob_ready")
        binv_ready = sem("binv_ready")
        pn_ready = sem("pn_ready")
        pnT_ps = sem("pnT_ps")
        pnT_ready = sem("pnT_ready")
        bo_ps = sem("bo_ps")
        bo_ready = sem("bo_ready")
        pT_ps = sem("pT_ps")
        pT_ready = sem("pT_ready")
        pple_ps = sem("pple_ps")
        pple_ready = sem("pple_ready")
        x2_ready = sem("x2_ready")
        h2T_ps = sem("h2T_ps")
        h2T_ready = sem("h2T_ready")
        logit_ps = sem("logit_ps")
        route = sem("route")
        route_exp = sem("route_exp")
        pos_ps = sem("pos_ps")
        npass_ready = sem("npass_ready")
        posm_step = sem("posm_step")
        gT_ps = sem("gT_ps")
        gT_ready = sem("gT_ready")
        yb_ps = sem("yb_ps")
        y_done = sem("y_done")
        sel_ready = sem("sel_ready")
        onehot_ready = sem("onehot_ready")
        ghot_ready = sem("ghot_ready")
        ghotT_ps = sem("ghotT_ps")
        ghotT_ready = sem("ghotT_ready")
        xg_ps = sem("xg_ps")
        xg_ready = sem("xg_ready")
        glu_ready = sem("glu_ready")
        lin_ready = sem("lin_ready")
        sig_ready = sem("sig_ready")
        gated_ready = sem("gated_ready")
        act_ready = sem("act_ready")
        actT_ps = sem("actT_ps")
        actT_ready = sem("actT_ready")
        out_s_ready = sem("out_s_ready")
        scatter_ps = sem("scatter_ps")
        fin_ps = sem("fin_ps")
        fin_sig = sem("fin_sig")
        fin_step = sem("fin_step")
        stored = sem("stored")

        w_in_k = w_in[0].rearrange("(k p) n -> p k n", p=P)
        w_out_k = w_out[0].rearrange("(k p) n -> p k n", p=P)
        w_pg_k = w_ple_gate[0].rearrange("(k p) n -> p k n", p=P)
        w_pp_k = w_ple_proj[0].rearrange("(k p) n -> p k n", p=P)
        gu_src = w_gate_up[0].rearrange("e (k p) n -> k p e n", p=P)
        dn_src = w_down[0].rearrange("e (j p f) n -> j p e (f n)", p=P, f=2)
        x_src = x[0].rearrange("(t p) d -> p t d", p=P)
        p_src = p[0, 0].rearrange("(t p) d -> p t d", p=P)
        out_dst = out[0].rearrange("(t p) d -> p t d", p=P)

        def slot(n, width, parts):
            return ring[:, n % RING, 0:parts * width].rearrange("p (k n) -> p k n", n=width)

        def wait_chunk(eng, n):
            eng.wait_ge(ring_full[n % RING], 16 * (n // RING + 1))

        block = ctx.enter_context(nc.Block())

        @block.sync
        def _(sp):
            sp.dma_start(xt[:], x_src).then_inc(x_loaded, 16)
            sp.wait_ge(zero_ready, 1)
            sp.dma_start(rows[0:1, :], mix_norm_g).then_inc(rows_loaded, 16)
            sp.dma_start(rows[1:2, :], ple_norm_g).then_inc(rows_loaded, 16)
            sp.dma_start(rows[2:2 + CONV, :], conv_w[0]).then_inc(rows_loaded, 16)
            sp.dma_start(rows[6:7, :], conv_b).then_inc(rows_loaded, 16)
            for r, g in ((7, q_norm_g), (8, k_norm_g)):
                for c in range(2):
                    sp.dma_start(rows[r:r + 1, c * DH:(c + 1) * DH], g).then_inc(rows_loaded, 16)
            sp.dma_start(w_if[:], w_in_k[:, :, IG:IG + 2 * H]).then_inc(small_loaded, 16)
            sp.dma_start(ig_bias[:], igate_b.rearrange("o h -> h o")).then_inc(small_loaded, 16)
            sp.dma_start(fg_bias[:], fgate_b.rearrange("o h -> h o")).then_inc(small_loaded, 16)

            def load(n, dst, src):
                if n >= RING:
                    sp.wait_ge(chunk_done, n - RING + 1)
                sp.dma_start(dst, src).then_inc(ring_full[n % RING], 16)

            for n in range(2):
                load(n, slot(n, NB, K), w_in_k[:, :, n * NB:(n + 1) * NB])
            sp.dma_start(pt_in[:], p_src).then_inc(late_loaded, 16)
            sp.dma_start(g_head[:], mlstm_head_g[0].rearrange("h d -> (h d)").rearrange("(o n) -> o n", o=1)
                         .to_broadcast([P, W])).then_inc(late_loaded, 16)
            for i, c0 in enumerate(SECTIONS):
                n = FIRST_SECTION + i
                load(n, slot(n, NB, K), w_in_k[:, :, c0:c0 + NB])
            sp.dma_start(g_ffn[:], ffn_norm_g.to_broadcast([P, D])).then_inc(late_loaded, 16)
            sp.dma_start(brb[:], b_router.to_broadcast([P, E])).then_inc(late_loaded, 16)
            sp.dma_start(w_r[:], w_router[0].rearrange("(k p) e -> p k e", p=P)).then_inc(late_loaded, 16)
            for j in range(4):
                sp.dma_start(bgu[32 * j:32 * j + E, :], b_gate_up[0][:, j * NB:(j + 1) * NB]).then_inc(late_loaded, 16)
            load(CHUNK_PLE, slot(CHUNK_PLE, D, PLE // P), w_pp_k)
            for c in range(2):
                load(CHUNK_WO + c, slot(CHUNK_WO + c, D, 4), w_out_k[:, 4 * c:4 * c + 4, :])

            def load_pair(it, pair):
                for c in range(PER_PAIR):
                    s = (MOE0 + c) % RING
                    sp.wait_ge(chunk_done, it * PER_PAIR + (MOE0 + c - RING + 1))
                    if c < K:
                        sp.dma_start(ring[:, s, :].rearrange("p (e n) -> p e n", e=2),
                                     gu_src[c, :, bass.ds(pair * 2, 2), :]).then_inc(ring_full[s], 16)
                    else:
                        j = c - K
                        sp.dma_start(ring[:, s, :].rearrange("p (e n) -> p e n", e=2),
                                     dn_src[j, :, bass.ds(pair * 2, 2), :]).then_inc(ring_full[s], 16)

            with sp.Fori(0, PAIRS) as pair:
                load_pair(pair, pair)
            sp.wait_ge(npass_ready, 1)
            npass = sp.value_load(npass_i[0:1, 0:1], min_val=1, max_val=S // SLOTS)
            with sp.If(npass > 1):
                with sp.Fori(1, npass) as ps:
                    with sp.Fori(0, PAIRS) as pair:
                        load_pair(ps * PAIRS + pair, pair)
            for c in range(2):
                s = (MOE0 + c) % RING
                sp.wait_ge(chunk_done, npass * (PER_PAIR * PAIRS) + (MOE0 + c - RING + 1))
                sp.dma_start(slot(MOE0 + c, D, 4), w_pg_k[:, 4 * c:4 * c + 4, :]).then_inc(ring_full[s], 16)
            for tt in range(TT):
                for n in range(HALVES):
                    sp.wait_ge(fin_step, 2 * (tt * HALVES + n) + 2)
                    sp.dma_start(out_dst[:, tt, n * NB:(n + 1) * NB], xs[:, tt, n * NB:(n + 1) * NB]).then_inc(stored, 16)
            sp.wait_ge(stored, 16 * TT * HALVES)

        @block.gpsimd
        def _(pool):
            g = nc.gpsimd
            g.memset(rows, 0.0).then_inc(zero_ready, 1)
            g.memset(ident[:], 0.0).then_inc(zero_ready, 1)
            g.memset(tri[:], 1.0).then_inc(zero_ready, 1)
            g.memset(before[:], 1.0).then_inc(zero_ready, 1)
            g.memset(sel_head[:], 0.0).then_inc(zero_ready, 1)
            pool.wait_ge(zero_ready, 5)
            g.affine_select(out=ident[:], in_=ident[:], compare_op=ALU.not_equal, fill=1.0, base=0,
                            pattern=[[-1, P]], channel_multiplier=1).then_inc(const_ready, 1)
            g.affine_select(out=tri[:], in_=tri[:], compare_op=ALU.is_ge, fill=0.0, base=0,
                            pattern=[[1, P]], channel_multiplier=-1).then_inc(const_ready, 1)
            g.affine_select(out=before[:], in_=before[:], compare_op=ALU.is_gt, fill=0.0, base=0,
                            pattern=[[1, P]], channel_multiplier=-1).then_inc(const_ready, 1)
            g.memset(ones[:], 1.0).then_inc(const_ready, 1)
            g.memset(zrow[:], 0.0).then_inc(const_ready, 1)
            g.affine_select(out=sel_head[:], in_=sel_head[:], compare_op=ALU.not_equal, fill=1.0, base=0,
                            pattern=[[-1, H], [0, P]], channel_multiplier=1).then_inc(const_ready, 1)
            g.memset(vx[:, :, :, DH:DH + 1], 1.0).then_inc(const_ready, 1)
            g.iota(dist[:, 0:P], pattern=[[1, P]], base=0, channel_multiplier=-1,
                   allow_small_or_imprecise_dtypes=True).then_inc(zero_ready, 1)
            g.iota(dist[:, P:TRI], pattern=[[1, S]], base=-P, channel_multiplier=-1,
                   allow_small_or_imprecise_dtypes=True).then_inc(zero_ready, 1)
            pool.wait_ge(zero_ready, 7)
            g.affine_select(out=dist[:, 0:P], in_=dist[:, 0:P], compare_op=ALU.is_ge, fill=MASKED, base=0,
                            pattern=[[-1, P]], channel_multiplier=1).then_inc(const_ready, 1)
            g.affine_select(out=dist[:, P:TRI], in_=dist[:, P:TRI], compare_op=ALU.is_ge, fill=MASKED, base=P,
                            pattern=[[-1, S]], channel_multiplier=1).then_inc(const_ready, 1)
            g.iota(iota_e[:], pattern=[[1, E]], base=0, channel_multiplier=0,
                   allow_small_or_imprecise_dtypes=True).then_inc(const_ready, 1)
            g.iota(iota_s[:], pattern=[[1, SLOTS]], base=0, channel_multiplier=0,
                   allow_small_or_imprecise_dtypes=True).then_inc(const_ready, 1)
            for h in range(H):
                pool.wait_ge(dmat_ready, h + 1)
                d = dmat[:, h % 2, :].rearrange("p (b s) -> p b s", b=3)[:, 0:3:2, :]
                g.tensor_tensor(d, d, tri[:].rearrange("p (o s) -> p o s", o=1).to_broadcast([P, 2, P]),
                                ALU.mult).then_inc(dmask_ready, 1)
            pool.wait_ge(late_loaded, LATE)
            for tt in range(TT):
                pool.wait_ge(og_ready, tt + 1)
                g.tensor_tensor(og[:, tt, :], og[:, tt, :], g_head[:], ALU.mult).then_inc(ogg_ready, 1)

            for tt in range(TT):
                pool.wait_ge(post_step, 4 + tt)
                g.tensor_tensor(hm[:, tt, W:2 * W], hm[:, tt, 0:W], hm[:, tt, 0:W], ALU.mult).then_inc(post_sq, 1)

            pool.wait_ge(x2_ready, 4)
            g.memset(sel_expert[:], 0.0).then_inc(zero_ready, 1)
            pool.wait_ge(zero_ready, 8)
            for j in range(4):
                v = sel_expert[32 * j:32 * j + 32]
                g.affine_select(out=v, in_=v, compare_op=ALU.not_equal, fill=1.0, base=0,
                                pattern=[[-1, E], [0, SLOTS]], channel_multiplier=1).then_inc(sel_built, 1)

        @block.tensor
        def _(pe):
            mm = nc.tensor.matmul
            tr = nc.tensor.transpose

            pe.wait_ge(const_ready, 1)
            pe.wait_ge(rows_loaded, 16 * 8)
            for k in range(K):
                last = tr(aux[:, 0, k * 9:(k + 1) * 9], rows[:, k * P:(k + 1) * P], ident[0:9, 0:9])
            last.then_inc(cols_ps, 1)

            def x_transposes(done):
                for j in range(K // 2):
                    bank = hu[:, 2 + j, :] if j < 2 else po[:, j - 2, :]
                    for k in (2 * j, 2 * j + 1):
                        for tt in range(TT):
                            c = (k % 2) * S + tt * P
                            last = tr(bank[:, c:c + P], xs[:, tt, k * P:(k + 1) * P], ident[:])
                    last.then_inc(done, 1)

            pe.wait_ge(xs_ready, TT)
            x_transposes(xT_ps)

            pe.wait_ge(hT_act, K // 2)
            pe.wait_ge(hT_dve, K // 2)
            pe.wait_ge(small_loaded, 16 * 3)
            for gi in range(2):
                for k in range(K):
                    last = mm(aux[0:H, 1, gi * S:(gi + 1) * S], w_if[:, k, gi * H:(gi + 1) * H], hT[:, k, :],
                              start=(k == 0), stop=(k == K - 1))
            last.then_inc(gate_ps, 1)

            for i in range(K):
                n, ct = divmod(i, 4)
                if ct == 0:
                    wait_chunk(pe, n)
                if i >= 2:
                    pe.wait_ge(conv_step, CONV * (i - 1))
                for k in range(K):
                    last = mm(hu[:, i % 2, 0:S], slot(n, NB, K)[:, k, ct * P:(ct + 1) * P], hT[:, k, :],
                              start=(k == 0), stop=(k == K - 1))
                last.then_inc(chunk_done if ct == 3 else qk_ps, 1)

            def half(sec, tt):
                n = FIRST_SECTION + sec
                if tt == 0:
                    wait_chunk(pe, n)
                if sec == SEC_V:
                    pe.wait_ge(conv_step, CONV * (K - 1 + tt))
                elif sec == SEC_Q:
                    pe.wait_ge(v_ready, tt + 1)
                elif sec in (SEC_K, SEC_MV):
                    pe.wait_ge(normed_ready, 2 * (sec - SEC_Q) - 1 + tt)
                else:
                    pe.wait_ge(vb_ready, tt + 1)
                for k in range(K):
                    last = mm(hu[:, tt, :], hT[:, k, tt * P:(tt + 1) * P], slot(n, NB, K)[:, k, :],
                              start=(k == 0), stop=(k == K - 1))
                last.then_inc(chunk_done if tt else half_ps, 1)

            for tt in range(TT):
                half(SEC_V, tt)

            pe.wait_ge(gate_step, GATE_STEPS)
            pe.wait_ge(cols_ready, 1)
            for c, src in enumerate((arow, negmt)):
                for tt in range(TT):
                    last = tr(aux[:, c, tt * H:(tt + 1) * H], src[:, tt * P:(tt + 1) * P],
                              ident[0:H, 0:H])
            last.then_inc(gcol_ps, 1)

            def head_rows(h):
                return slice(DH * (h % 2), DH * (h % 2) + DH)

            def mlstm_scores(h):
                if h == 0:
                    pe.wait_ge(qk_ready, K)
                    pe.wait_ge(hT_act, K // 2)
                    pe.wait_ge(hT_dve, K // 2)
                    pe.wait_ge(const_ready, 7)
                if h >= 2:
                    pe.wait_ge(smat_ready, h - 1)
                mm(hu[:, 2, (h % 2) * S:(h % 2) * S + S], sel_head[:, h, :], negm[:], start=True, stop=True)
                r = head_rows(h)
                q, k = qkT[r, h // 2, :], qkT[r, 4 + h // 2, :]
                mm(po[:, h % 2, 0:S], k[:, 0:P], q, start=True, stop=True)
                mm(po[:, h % 2, S:TRI], k[:, P:S], q[:, P:S], start=True, stop=True).then_inc(mscore_ps, 1)

            def mlstm_num(h):
                pe.wait_ge(smat_ready, h + 1)
                if h == 0:
                    pe.wait_ge(v_ready, TT)
                if h >= 1:
                    pe.wait_ge(num_ready, h)
                c = (h % 2) * S
                s = smat[:, h % 2, :]
                n = DH + 1
                mm(hu[:, 3, c:c + n], s[:, 0:P], vx[:, 0, h, :], start=True, stop=True)
                mm(hu[:, 3, c + n:c + 2 * n], s[:, P:S], vx[:, 0, h, :], start=True, stop=False)
                mm(hu[:, 3, c + n:c + 2 * n], s[:, S:TRI], vx[:, 1, h, :], start=False, stop=True).then_inc(num_ps, 1)

            def norm_transposes(i):
                pe.wait_ge(normed_ready, i + 1)
                if i >= 2:
                    pe.wait_ge(bqT_ready, i - 1)
                elif i == 0:
                    pe.wait_ge(emc_ready, 1)
                    pe.wait_ge(acol_ready, 1)
                for j in range(4):
                    last = tr(aux[:, i % 2, j * P:(j + 1) * P], normed[:, i % 2, j * P:(j + 1) * P], ident[:])
                last.then_inc(normT_ps, 1)

            pe.wait_ge(gate_step, GATE_STEPS)
            for h in range(H):
                mlstm_scores(h)
                half(SEC_Q + h // 2, h % 2)
                mlstm_num(h)
                if 1 <= h <= 4:
                    norm_transposes(h - 1)

            pe.wait_ge(late_loaded, LATE)
            pe.wait_ge(bqT_ready, 4)
            for k in range(PLE // P):
                for tt in range(TT):
                    last = tr(aux[:, 0, k * S + tt * P:k * S + tt * P + P], pt_in[:, tt, k * P:(k + 1) * P], ident[:])
            last.then_inc(pT_ps, 1)
            wait_chunk(pe, CHUNK_PLE)
            pe.wait_ge(pT_ready, 1)
            pe.wait_ge(og_ready, TT)
            pe.wait_ge(num_ready, H)
            for tt in range(TT):
                for n in range(HALVES):
                    for k in range(PLE // P):
                        last = mm(hu[:, tt * 2 + n, :], pT[:, k, tt * P:(tt + 1) * P],
                                  slot(CHUNK_PLE, D, 2)[:, k, n * NB:(n + 1) * NB], start=(k == 0), stop=(k == 1))
                    if tt * 2 + n < 3:
                        last.then_inc(pple_ps, 1)
            last.then_inc(chunk_done, 1)

            def moba_scores(h):
                if h == 0:
                    pe.wait_ge(smat_ready, H)
                if h >= 2:
                    pe.wait_ge(bias_ready, h - 1)
                r = head_rows(h)
                q, k = bqT[r, h // 2, :], bqT[r, 4 + h // 2, :]
                mm(po[:, h % 2, 0:P], q[:, 0:P], k[:, 0:P], start=True, stop=True)
                mm(po[:, h % 2, P:TRI], q[:, P:S], k, start=True, stop=True).then_inc(bscore_ps, 1)

            def moba_transposes(h):
                pe.wait_ge(pn_ready, 2 * h + 2)
                if h >= 1:
                    pe.wait_ge(pnT_ready, h)
                for b in range(3):
                    last = tr(aux[:, 0, b * P:(b + 1) * P], smat[:, h % 2, b * P:(b + 1) * P], ident[:])
                last.then_inc(pnT_ps, 1)

            def moba_values(h):
                pe.wait_ge(pnT_ready, h + 1)
                if h == 0:
                    pe.wait_ge(vb_ready, TT)
                if h % 2 == 0 and h >= 2:
                    pe.wait_ge(bo_ready, h // 2)
                r = head_rows(h)
                v = vb[:, :, h * DH:(h + 1) * DH]
                mm(aux[r, 1, 0:S], v[:, 0, :], dmat[:, h % 2, 0:S], start=True, stop=False)
                mm(aux[r, 1, P:S], v[:, 1, :], dmat[:, h % 2, S:TRI], start=False, stop=True).then_inc(bo_ps, 1)

            def mix_out(ks, done=None):
                for k in ks:
                    n = CHUNK_WO + k // 4
                    for tt in range(TT):
                        for b in range(HALVES):
                            last = mm(hu[:, tt * 2 + b, :], mixT[:, k, tt * P:(tt + 1) * P],
                                      slot(n, D, 4)[:, k % 4, b * NB:(b + 1) * NB], start=(k == 0), stop=(k == K - 1))
                    if k % 4 == 3:
                        last.then_inc(chunk_done, 1)

            moba_scores(0)
            moba_scores(1)
            pe.wait_ge(hm_ready, TT)
            pe.wait_ge(pple_ready, 4)
            for tt in range(TT):
                for j in range(4):
                    last = tr(hu[:, tt, j * P:(j + 1) * P], hm[:, tt, j * P:(j + 1) * P], ident[:])
                last.then_inc(hmT_ps, 1)
            for h in range(H):
                moba_transposes(h)
                if h == 1:
                    wait_chunk(pe, CHUNK_WO)
                    pe.wait_ge(hmT_ready, TT)
                if 1 <= h <= 4:
                    mix_out([h - 1])
                moba_values(h)
                if h + 2 < H:
                    moba_scores(h + 2)
            wait_chunk(pe, CHUNK_WO + 1)
            pe.wait_ge(bo_ready, H // 2)
            mix_out(range(4, K))

            pe.wait_ge(xs_ready, 2 * TT)
            x_transposes(h2T_ps)
            pe.wait_ge(h2T_ready, K // 2)
            for tt in range(TT):
                for k in range(K):
                    last = mm(aux[:, 0, tt * E:(tt + 1) * E], hT[:, k, tt * P:(tt + 1) * P], w_r[:, k, :],
                              start=(k == 0), stop=(k == K - 1))
            last.then_inc(logit_ps, 1)
            pe.wait_ge(route, ROUTE_MASK)
            mm(aux[:, 1, 0:E], before[:], mask[:, 0, :], start=True, stop=True)
            mm(aux[:, 1, E:2 * E], ones[:], mask[:, 0, :], start=True, stop=False)
            mm(aux[:, 1, E:2 * E], before[:], mask[:, 1, :], start=False, stop=True)
            mm(aux[:, 1, 2 * E:3 * E], ones[:], mask[:, 0, :], start=True, stop=False)
            mm(aux[:, 1, 2 * E:3 * E], ones[:], mask[:, 1, :], start=False, stop=True).then_inc(pos_ps, 1)
            pe.wait_ge(route, ROUTE_GATES)
            for tt in range(TT):
                last = tr(po[0:E, 0, tt * P:(tt + 1) * P], gates[:, tt, :], ident[:])
            last.then_inc(gT_ps, 1)
            pe.wait_ge(gT_ready, 1)
            pe.wait_ge(bdn_loaded, 16)
            for tt in range(TT):
                for n in range(HALVES):
                    last = mm(hu[:, tt * 2 + n, :], gT[:, tt * P:(tt + 1) * P], bdn[:, n * NB:(n + 1) * NB],
                              start=True, stop=True)
            last.then_inc(yb_ps, 1)

            def gather():
                for k in range(K):
                    for tt in range(TT):
                        last = mm(aux[:, k // 4, (k % 4) * P:(k % 4 + 1) * P], h2[:, tt, k * P:(k + 1) * P],
                                  onehot[:, tt, :, :].rearrange("p e s -> p (e s)"), start=(tt == 0), stop=(tt == TT - 1))
                last.then_inc(xg_ps, 1)

            pe.wait_ge(onehot_ready, 1)
            gather()

            pe.wait_ge(npass_ready, 1)
            npass = pe.value_load(npass_i[0:1, 0:1], min_val=1, max_val=S // SLOTS)
            with pe.Fori(0, npass) as ps:
                with pe.Fori(0, PAIRS) as pair:
                    it = ps * PAIRS + pair
                    pe.wait_ge(ghot_ready, it + 1)
                    pe.wait_ge(xg_ready, it * 2 + 2)
                    for tt in range(TT):
                        last = tr(aux[:, 0, tt * P:(tt + 1) * P], ghot[:, tt, :, :].rearrange("p e s -> p (e s)"), ident[:])
                    last.then_inc(ghotT_ps, 1)
                    pe.wait_ge(sel_ready, it + 1)
                    pe.wait_ge(y_done, it * 4 + 4)
                    for j in range(4):
                        mm(hu[:, j, :], sel[32 * j:32 * j + E, :], bgu[32 * j:32 * j + E, :], start=True, stop=False, skip_group_check=True)
                    for k in range(K):
                        s = (MOE0 + k) % RING
                        pe.wait_ge(ring_full[s], it * 32 + 16 * ((MOE0 + k) // RING + 1))
                        for j in range(4):
                            for e in range(2):
                                last = mm(hu[e * SLOTS:(e + 1) * SLOTS, j, :], xg[:, k, e * SLOTS:(e + 1) * SLOTS],
                                          ring[:, s, e * 2048 + j * NB:e * 2048 + (j + 1) * NB],
                                          start=False, stop=(k == K - 1), skip_group_check=True)
                        last.then_inc(chunk_done, 1)
                    pe.wait_ge(onehot_ready, it + 2)
                    pe.wait_ge(ghotT_ready, it + 1)
                    gather()
                    pe.wait_ge(xg_ready, it * 2 + 4)
                    for c in range(2):
                        pe.wait_ge(act_ready, it * 2 + (c + 1))
                        for b in range(4):
                            c0 = (2 * c + b // 2) * 2 * P + b % 2
                            last = tr(aux[:, c, b * P:(b + 1) * P], act_s[:, c0:c0 - b % 2 + 2 * P:2], ident[:])
                        last.then_inc(actT_ps, 1)
                    for j in range(K // 2):
                        c = K + j
                        s = (MOE0 + c) % RING
                        if j % 2 == 0:
                            pe.wait_ge(actT_ready, it * 2 + (j // 2 + 1))
                        pe.wait_ge(ring_full[s], it * 32 + 16 * ((MOE0 + c) // RING + 1))
                        for f in range(2):
                            for n in range(HALVES):
                                for e in range(2):
                                    o = (e * 2 + f) * D + n * NB
                                    last = mm(po[e * SLOTS:(e + 1) * SLOTS, n, :],
                                              actT[:, 2 * j + f, e * SLOTS:(e + 1) * SLOTS], ring[:, s, o:o + NB],
                                              start=(j == 0 and f == 0), stop=(j == K // 2 - 1 and f == 1),
                                              skip_group_check=True)
                        last.then_inc(chunk_done, 1)
                    for n in range(HALVES):
                        pe.wait_ge(out_s_ready, it * 2 + (n + 1))
                        for tt in range(TT):
                            last = mm(hu[:, tt * 2 + n, :], ghotT[:, tt * P:(tt + 1) * P], out_s[:, n * NB:(n + 1) * NB],
                                      start=True, stop=True)
                    last.then_inc(scatter_ps, 1)

            pe.wait_ge(xs_ready, 3 * TT)
            x_transposes(xT_ps)
            pe.wait_ge(hT_act, K)
            pe.wait_ge(hT_dve, K)
            for c in range(2):
                s = (MOE0 + c) % RING
                pe.wait_ge(ring_full[s], npass * (PAIRS * 32) + 16 * ((MOE0 + c) // RING + 1))
            for tt in range(TT):
                for n in range(HALVES):
                    for k in range(K):
                        last = mm(hu[:, tt * 2 + n, :], hT[:, k, tt * P:(tt + 1) * P],
                                  slot(MOE0 + k // 4, D, 4)[:, k % 4, n * NB:(n + 1) * NB],
                                  start=(k == 0), stop=(k == K - 1))
                    last.then_inc(fin_ps, 1)

        @block.vector
        def _(dve):
            v = nc.vector

            def norm(phase, gain):
                st = stat[:, 8 * phase:8 * phase + 8]
                dve.wait_ge(ss_ready, TT * (phase + 1))
                v.tensor_scalar(st[:, 2:4], st[:, 0:2], 1.0 / D, EPS, ALU.mult, ALU.add).then_inc(rstd_step, 1)
                dve.wait_ge(root_ready, phase + 1)
                v.reciprocal(st[:, 6:8], st[:, 4:6]).then_inc(rstd_step, 1)
                dve.wait_ge(rstd_step, 2 * phase + 2)
                for tt in range(TT):
                    r = st[:, 6 + tt:7 + tt]
                    if gain is None:
                        ins = v.tensor_scalar(xs[:, tt, :], xt[:, tt, :], r, None, ALU.mult)
                    else:
                        ins = v.scalar_tensor_tensor(out=xs[:, tt, :], in0=xt[:, tt, :], scalar=r, in1=gain[:],
                                                     op0=ALU.mult, op1=ALU.mult)
                    ins.then_inc(xs_ready, 1)

            def hT_upper(count, row):
                for k in range(4, K):
                    dve.wait_ge(xT_ps, count + k // 2 + 1)
                    v.tensor_scalar(hT[:, k, :], po[:, k // 2 - 2, (k % 2) * S:(k % 2) * S + S],
                                    cols[:, k, row:row + 1], None, ALU.mult).then_inc(hT_dve, 1)

            norm(0, None)
            dve.wait_ge(cols_ps, 1)
            v.tensor_copy(cols[:].rearrange("p k r -> p (k r)"), aux[:, 0, 0:K * 9]).then_inc(cols_ready, 1)
            dve.wait_ge(cols_ready, 1)
            hT_upper(0, 0)

            dve.wait_ge(gate_ps, 1)
            dve.wait_ge(const_ready, 7)
            n = [0]

            def gate(ins):
                n[0] += 1
                ins.then_inc(gate_step, 1)
                dve.wait_ge(gate_step, n[0])

            gate(v.tensor_scalar(fpre, aux[0:H, 1, S:2 * S], fg_bias[:, 0:1], None, ALU.add))
            gate(v.tensor_scalar(fneg, fpre, -1.0, None, ALU.mult))
            gate(v.tensor_tensor(fneg, fneg, fpre, ALU.min))
            gate(v.tensor_scalar(fpre, fpre, 0.0, None, ALU.min))
            dve.wait_ge(gate_act, 2)
            gate(v.tensor_tensor(fpre, fpre, fln, ALU.subtract))
            gate(v.tensor_tensor_scan(blog, zrow[:], fpre, 0.0, ALU.add, ALU.add))
            gate(v.scalar_tensor_tensor(out=arow[:], in0=aux[0:H, 1, 0:S], scalar=ig_bias[:, 0:1], in1=blog,
                                        op0=ALU.add, op1=ALU.subtract))
            gate(v.tensor_tensor_scan(mrow[:], zrow[:], arow[:], 0.0, ALU.add, ALU.max))
            gate(v.tensor_scalar(negm[:], mrow[:], -1.0, None, ALU.mult))
            gate(v.scalar_tensor_tensor(out=negmt[:], in0=mrow[:], scalar=-1.0, in1=blog,
                                        op0=ALU.mult, op1=ALU.subtract))

            for i in range(K):
                nq, ct = divmod(i, 4)
                if ct == 3:
                    dve.wait_ge(chunk_done, nq + 1)
                else:
                    dve.wait_ge(qk_ps, 3 * nq + ct + 1)
                src = hu[:, i % 2, 0:S]
                v.tensor_scalar(qkT[:, i, :], src, cols[:, i, 5:6], cols[:, i, 6:7], ALU.mult, ALU.add)\
                 .then_inc(conv_step, 1)
                for back in range(1, CONV):
                    dve.wait_ge(conv_step, CONV * i + back)
                    v.scalar_tensor_tensor(out=qkT[:, i, back:S], in0=src[:, 0:S - back],
                                           scalar=cols[:, i, 5 - back:6 - back], in1=qkT[:, i, back:S],
                                           op0=ALU.mult, op1=ALU.add).then_inc(conv_step, 1)

            dve.wait_ge(gcol_ps, 1)
            v.tensor_copy(acol[:].rearrange("p t h -> p (t h)"), aux[:, 0, 0:TT * H]).then_inc(acol_ready, 1)
            dve.wait_ge(acol_ready, 1)

            def normed_half(i):
                sec, tt = SEC_Q + i // 2, i % 2
                ss = small[:, 0:H]
                dve.wait_ge(sq_ready, i + 1)
                v.tensor_reduce(ss, xs[:, tt, 0:W].rearrange("p (h d) -> p h d", h=H), AX.X, ALU.add).then_inc(nstat, 1)
                dve.wait_ge(nstat, 3 * i + 1)
                v.tensor_scalar(small[:, H:2 * H], ss, 1.0 / DH, EPS, ALU.mult, ALU.add).then_inc(nstat, 1)
                dve.wait_ge(nroot, i + 1)
                v.reciprocal(small[:, 3 * H:4 * H], small[:, 2 * H:3 * H]).then_inc(nstat, 1)
                dve.wait_ge(nstat, 3 * i + 3)
                if i >= 2:
                    dve.wait_ge(normT_ps, i - 1)
                v.tensor_tensor(normed[:, i % 2, :].rearrange("p (h d) -> p h d", h=H),
                                hu[:, tt, :].rearrange("p (h d) -> p h d", h=H),
                                small[:, 3 * H:4 * H].rearrange("p (h o) -> p h o", o=1).to_broadcast([P, H, DH]),
                                ALU.mult).then_inc(normed_ready, 1)

            def normed_transposed(i):
                dve.wait_ge(normT_ps, i + 1)
                j, tt = 4 * (i // 2), i % 2
                v.tensor_scalar(bqT[:, j:j + 4, tt * P:(tt + 1) * P],
                                aux[:, i % 2, :].rearrange("p (j t) -> p j t", j=4),
                                cols[:, 0, 7 + i // 2:8 + i // 2], DH ** -0.5 if i < 2 else 1.0,
                                ALU.mult, ALU.mult).then_inc(bqT_ready, 1)

            for h in range(H):
                dve.wait_ge(mscore_ps, h + 1)
                b = hu[:, 2, (h % 2) * S:(h % 2) * S + S]
                v.tensor_scalar(expo[:, h % 2, 0:S], b, acol[:, 0, h:h + 1], 0.0, ALU.add, ALU.min)\
                 .then_inc(expo_ready, 1)
                v.tensor_scalar(expo[:, h % 2, S:TRI], b[:, P:S], acol[:, 1, h:h + 1], 0.0, ALU.add, ALU.min)\
                 .then_inc(expo_ready, 1)
                dve.wait_ge(dmask_ready, h + 1)
                if h >= 2:
                    dve.wait_ge(num_ps, h - 1)
                v.scalar_tensor_tensor(out=smat[:, h % 2, :], in0=po[:, h % 2, 0:TRI], scalar=DH ** -0.5,
                                       in1=dmat[:, h % 2, :], op0=ALU.mult, op1=ALU.mult).then_inc(smat_ready, 1)
                if h < 4:
                    normed_half(h)
                if 1 <= h <= 4:
                    normed_transposed(h - 1)

            post = [0]

            def step(ins):
                post[0] += 1
                ins.then_inc(post_step, 1)
                dve.wait_ge(post_step, post[0])

            def stat16(c):
                return small[:, 64 + c * TT * H:64 + (c + 1) * TT * H]

            def by_tt(c):
                return stat16(c).rearrange("p (t h) -> p t h", t=TT)

            def head_scale(c, tt):
                return stat16(c)[:, tt * H:(tt + 1) * H].rearrange("p (h o) -> p h o", o=1).to_broadcast([P, H, DH])

            dve.wait_ge(num_ready, H)
            dve.wait_ge(emc_ready, 1)
            den = num[:, :, :, DH]
            step(v.scalar_tensor_tensor(out=by_tt(0), in0=den, scalar=-1.0, in1=den, op0=ALU.mult, op1=ALU.max))
            step(v.tensor_tensor(by_tt(0), by_tt(0), emc[:], ALU.max))
            step(v.reciprocal(stat16(1), stat16(0)))
            for tt in range(TT):
                h3 = hm[:, tt, 0:W].rearrange("p (h d) -> p h d", h=H)
                step(v.tensor_tensor(h3, num[:, tt, :, 0:DH], head_scale(1, tt), ALU.mult))
            for tt in range(TT):
                dve.wait_ge(post_sq, tt + 1)
                step(v.tensor_reduce(by_tt(2)[:, tt, :], hm[:, tt, W:2 * W].rearrange("p (h d) -> p h d", h=H),
                                     AX.X, ALU.add))
            step(v.tensor_scalar(stat16(3), stat16(2), 1.0 / DH, EPS, ALU.mult, ALU.add))
            dve.wait_ge(post_act, 1)
            step(v.reciprocal(stat16(5), stat16(4)))
            for tt in range(TT):
                h3 = hm[:, tt, 0:W].rearrange("p (h d) -> p h d", h=H)
                step(v.tensor_tensor(h3, h3, head_scale(5, tt), ALU.mult))
                dve.wait_ge(ogg_ready, tt + 1)
                v.tensor_tensor(hm[:, tt, 0:W], hm[:, tt, 0:W], og[:, tt, :], ALU.mult).then_inc(hm_ready, 1)

            def moba_max(h):
                dve.wait_ge(bscore_ps, h + 1)
                slope = 2.0 ** (-8.0 * (h + 1) / H)
                b = expo[:, h % 2, :]
                v.scalar_tensor_tensor(out=b, in0=dist[:], scalar=slope, in1=po[:, h % 2, 0:TRI],
                                       op0=ALU.mult, op1=ALU.add).then_inc(bias_ready, 1)
                dve.wait_ge(bias_ready, h + 1)
                v.tensor_reduce(negmax[:, h % 2, 0:1], b[:, 0:P], AX.X, ALU.max, negate=True).then_inc(bmax_ready, 1)
                v.tensor_reduce(negmax[:, h % 2, 1:2], b[:, P:TRI], AX.X, ALU.max, negate=True).then_inc(bmax_ready, 1)

            moba_max(0)
            moba_max(1)
            for tt in range(TT):
                dve.wait_ge(hmT_ps, tt + 1)
                v.tensor_copy(mixT[:, 0:4, tt * P:(tt + 1) * P], hu[:, tt, :].rearrange("p (j t) -> p j t", j=4))\
                 .then_inc(hmT_ready, 1)
            for h in range(H):
                dve.wait_ge(prob_ready, 2 * h + 2)
                inv = small[:, 48 + 2 * (h % 2):50 + 2 * (h % 2)]
                v.reciprocal(inv, psum_[:, h % 2, :]).then_inc(binv_ready, 1)
                dve.wait_ge(binv_ready, h + 1)
                for tt, (lo, hi) in enumerate(((0, P), (P, TRI))):
                    v.tensor_scalar(smat[:, h % 2, lo:hi], smat[:, h % 2, lo:hi], inv[:, tt:tt + 1], None,
                                    ALU.mult).then_inc(pn_ready, 1)
                if h + 2 < H:
                    moba_max(h + 2)

            dve.wait_ge(chunk_done, CHUNK_WO + 2)
            for tt in range(TT):
                for b in range(HALVES):
                    q = xt[:, tt, b * NB:(b + 1) * NB]
                    v.tensor_tensor(q, q, hu[:, tt * 2 + b, :], ALU.add).then_inc(x2_ready, 1)
            dve.wait_ge(x2_ready, 4)
            dve.wait_ge(late_loaded, LATE)
            norm(1, g_ffn)
            for j in (2, 3):
                dve.wait_ge(h2T_ps, j + 1)
                v.tensor_copy(hT[:, 2 * j:2 * j + 2, :].rearrange("p k s -> p (k s)"), po[:, j - 2, :])\
                 .then_inc(h2T_ready, 1)

            steps = [0]

            def routed(ins, wait=True):
                steps[0] += 1
                ins.then_inc(route, 1)
                if wait:
                    dve.wait_ge(route, steps[0])

            dve.wait_ge(logit_ps, 1)
            for tt in range(TT):
                routed(v.tensor_tensor(lg[:, tt, :], aux[:, 0, tt * E:(tt + 1) * E], brb[:], ALU.add), tt == 1)
            for tt in range(TT):
                routed(v.max(top[:, tt, :], lg[:, tt, :]), tt == 1)
            for tt in range(TT):
                routed(v.max_index(topi[:, tt, :], top[:, tt, :], lg[:, tt, :]), tt == 1)
            routed(v.tensor_copy(topf[:], topi[:]))
            for tt in range(TT):
                routed(v.tensor_tensor(eq[:, tt, :, :],
                                       iota_e[:].rearrange("p (e o) -> p e o", o=1).to_broadcast([P, E, TOP_K]),
                                       topf[:, tt, 0:TOP_K].rearrange("p (o k) -> p o k", o=1).to_broadcast([P, E, TOP_K]),
                                       ALU.is_equal), tt == 1)
            routed(v.tensor_reduce(mask[:].rearrange("p t e -> p (t e)"), eq[:].rearrange("p t e k -> p (t e) k"),
                                   AX.X, ALU.add))
            assert steps[0] == ROUTE_MASK
            routed(v.tensor_scalar(stat[:, 32:34], top[:, :, 0], -1.0, None, ALU.mult))
            dve.wait_ge(route_exp, TT)
            routed(v.tensor_tensor(gates[:], gates[:], mask[:], ALU.mult))
            routed(v.tensor_reduce(stat[:, 34:36], gates[:], AX.X, ALU.add))
            routed(v.reciprocal(stat[:, 36:38], stat[:, 34:36]))
            for tt in range(TT):
                routed(v.tensor_scalar(gates[:, tt, :], gates[:, tt, :], stat[:, 36 + tt:37 + tt], None, ALU.mult), tt == 1)
            assert steps[0] == ROUTE_GATES
            dve.wait_ge(pos_ps, 1)
            routed(v.scalar_tensor_tensor(out=posm[:, :, 0:E], in0=aux[:, 1, 0:TT * E].rearrange("p (t e) -> p t e", t=TT),
                                          scalar=1.0, in1=mask[:], op0=ALU.add, op1=ALU.mult))
            routed(v.tensor_scalar(posm[:, :, 0:E], posm[:, :, 0:E], -1.0, None, ALU.add))
            routed(v.tensor_scalar(posm[:, :, E:E + 2], posm[:, :, 0:2], -float(SLOTS), None, ALU.add))

            def one_hot(first):
                v.tensor_tensor(onehot, iota_s[:].rearrange("p (a b s) -> p a b s", a=1, b=1).to_broadcast([P, TT, 2, SLOTS]),
                                posm[:, :, first].rearrange("p t (e o) -> p t e o", o=1).to_broadcast([P, TT, 2, SLOTS]),
                                ALU.is_equal).then_inc(onehot_ready, 1)

            routed(v.tensor_reduce(cnt[:, 0:1], aux[:, 1, 2 * E:3 * E], AX.X, ALU.max))
            one_hot(slice(0, 2))
            for j in range(1, S // SLOTS):
                routed(v.tensor_scalar(cnt[:, j:j + 1], cnt[:, 0:1], float(j * SLOTS), None, ALU.is_gt), j == 3)
            routed(v.tensor_reduce(cnt[:, 4:5], cnt[:, 1:4], AX.X, ALU.add))
            v.tensor_scalar(npass_i[:], cnt[0:1, 4:5], 1.0, None, ALU.add).then_inc(npass_ready, 1)
            dve.wait_ge(yb_ps, 1)

            def add_y():
                for tt in range(TT):
                    for b in range(HALVES):
                        q = xt[:, tt, b * NB:(b + 1) * NB]
                        v.tensor_tensor(q, q, hu[:, tt * 2 + b, :], ALU.add).then_inc(y_done, 1)

            add_y()
            dve.wait_ge(npass_ready, 1)
            npass = dve.value_load(npass_i[0:1, 0:1], min_val=1, max_val=S // SLOTS)
            with dve.Fori(0, npass) as ps:
                with dve.Fori(0, PAIRS) as pair:
                    it = ps * PAIRS + pair
                    dve.wait_ge(sel_built, 4)
                    v.tensor_copy(sel.rearrange("p (e s) -> p e s", e=2), sel_expert[:, bass.ds(pair * 2, 2), :])\
                     .then_inc(sel_ready, 1)
                    dve.wait_ge(onehot_ready, it + 1)
                    gp = gates[:, :, bass.ds(pair * 2, 2)]
                    v.tensor_tensor(ghot, onehot, gp.rearrange("p t (e o) -> p t e o", o=1)
                                    .to_broadcast([P, TT, 2, SLOTS]), ALU.mult).then_inc(ghot_ready, 1)
                    dve.wait_ge(ghot_ready, it + 1)
                    dve.wait_ge(xg_ps, it + 1)
                    one_hot(bass.ds(pair * 2 + 2, 2))
                    dve.wait_ge(chunk_done, it * PER_PAIR + (MOE0 + K))
                    for c in range(2):
                        v.tensor_scalar(glu[:, c * NB:(c + 1) * NB], hu[:, c, :], LIMIT, None, ALU.min)\
                         .then_inc(glu_ready, 1)
                    for c in range(2):
                        v.tensor_scalar(lin[:, c * NB:(c + 1) * NB], hu[:, 2 + c, :], LIMIT, -LIMIT, ALU.min, ALU.max)\
                         .then_inc(lin_ready, 1)
                    dve.wait_ge(lin_ready, it * 2 + 2)
                    for c in range(2):
                        q = slice(c * NB, (c + 1) * NB)
                        dve.wait_ge(sig_ready, it * 2 + (c + 1))
                        v.tensor_tensor(glu[:, q], glu[:, q], sig[:, q], ALU.mult).then_inc(gated_ready, 1)
                        dve.wait_ge(gated_ready, it * 2 + (c + 1))
                        v.scalar_tensor_tensor(out=act_s[:, q], in0=lin[:, q], scalar=1.0, in1=glu[:, q],
                                               op0=ALU.add, op1=ALU.mult).then_inc(act_ready, 1)
                    dve.wait_ge(scatter_ps, it + 1)
                    dve.wait_ge(y_done, it * 4 + 4)
                    add_y()
                dve.wait_ge(onehot_ready, ps * PAIRS + (PAIRS + 1))
                v.tensor_scalar(posm[:], posm[:], -float(SLOTS), None, ALU.add).then_inc(posm_step, 1)
                dve.wait_ge(posm_step, ps + 1)

            dve.wait_ge(y_done, npass * (PAIRS * 4) + 4)
            norm(2, None)
            hT_upper(K // 2, 1)
            for i in range(TT * HALVES):
                tt, b = divmod(i, HALVES)
                q = slice(b * NB, (b + 1) * NB)
                dve.wait_ge(fin_sig, i + 1)
                v.tensor_tensor(xs[:, tt, q], lin2[:, tt, q], pple[:, tt, q], ALU.mult).then_inc(fin_step, 1)
                dve.wait_ge(fin_step, 2 * i + 1)
                v.tensor_tensor(xs[:, tt, q], xs[:, tt, q], xt[:, tt, q], ALU.add).then_inc(fin_step, 1)

        @block.scalar
        def _(act):
            a = nc.scalar

            def squares(phase):
                st = stat[:, 8 * phase:8 * phase + 8]
                junk = xs if phase != 2 else big2[:].rearrange("p (t d) -> p t d", t=TT)
                for tt in range(TT):
                    a.activation(junk[:, tt, :], xt[:, tt, :], ACT.Square, accum_out=st[:, tt:tt + 1])\
                     .then_inc(ss_ready, 1)
                act.wait_ge(rstd_step, 2 * phase + 1)
                a.activation(st[:, 4:6], st[:, 2:4], ACT.Sqrt).then_inc(root_ready, 1)

            def hT_lower(count, row):
                for k in range(4):
                    act.wait_ge(xT_ps, count + k // 2 + 1)
                    a.activation(hT[:, k, :], hu[:, 2 + k // 2, (k % 2) * S:(k % 2) * S + S], ACT.Copy,
                                 scale=cols[:, k, row:row + 1]).then_inc(hT_act, 1)

            act.wait_ge(x_loaded, 16)
            squares(0)
            act.wait_ge(cols_ready, 1)
            hT_lower(0, 0)
            act.wait_ge(gate_step, 3)
            a.activation(fln, fneg, ACT.Exp).then_inc(gate_act, 1)
            act.wait_ge(gate_act, 1)
            a.activation(fln, fln, ACT.Ln, bias=1.0).then_inc(gate_act, 1)
            for i in range(K):
                act.wait_ge(conv_step, CONV * (i + 1))
                a.activation(qkT[:, i, :], qkT[:, i, :], ACT.Silu).then_inc(qk_ready, 1)

            def wait_half(sec, tt):
                if tt == 0:
                    act.wait_ge(half_ps, sec + 1)
                else:
                    act.wait_ge(chunk_done, FIRST_SECTION + sec + 1)

            act.wait_ge(const_ready, 7)
            for tt in range(TT):
                wait_half(SEC_V, tt)
                a.copy(vx[:, tt, :, 0:DH], hu[:, tt, :].rearrange("p (h d) -> p h d", h=H)).then_inc(v_ready, 1)
            act.wait_ge(gcol_ps, 1)
            a.activation(emc[:].rearrange("p t h -> p (t h)"), aux[:, 1, 0:TT * H], ACT.Exp)\
             .then_inc(emc_ready, 1)
            for h in range(H):
                act.wait_ge(expo_ready, 2 * h + 2)
                a.activation(dmat[:, h % 2, :], expo[:, h % 2, :], ACT.Exp).then_inc(dmat_ready, 1)
                sec, tt = SEC_Q + h // 2, h % 2
                wait_half(sec, tt)
                if h < 4:
                    if h >= 2:
                        act.wait_ge(nstat, 3 * (h - 2) + 1)
                    a.activation(xs[:, tt, 0:W], hu[:, tt, :], ACT.Square).then_inc(sq_ready, 1)
                    act.wait_ge(nstat, 3 * h + 2)
                    a.activation(small[:, 2 * H:3 * H], small[:, H:2 * H], ACT.Sqrt).then_inc(nroot, 1)
                elif sec == SEC_MV:
                    a.copy(vb[:, tt, :], hu[:, tt, :]).then_inc(vb_ready, 1)
                else:
                    a.activation(og[:, tt, :], hu[:, tt, :], ACT.Sigmoid).then_inc(og_ready, 1)
                act.wait_ge(num_ps, h + 1)
                c = (h % 2) * S
                a.copy(num[:, :, h, :], hu[:, 3, c:c + 2 * (DH + 1)].rearrange("p (t d) -> p t d", t=TT))\
                 .then_inc(num_ready, 1)
            act.wait_ge(pT_ps, 1)
            a.copy(pT[:].rearrange("p k s -> p (k s)"), aux[:, 0, :]).then_inc(pT_ready, 1)
            for i in range(TT * HALVES):
                if i < 3:
                    act.wait_ge(pple_ps, i + 1)
                else:
                    act.wait_ge(chunk_done, CHUNK_PLE + 1)
                a.copy(pple[:, i // 2, (i % 2) * NB:(i % 2 + 1) * NB], hu[:, i, :]).then_inc(pple_ready, 1)
            act.dma_start(bdn, b_down[0]).then_inc(bdn_loaded, 16)
            act.wait_ge(post_step, 8)
            a.activation(small[:, 64 + 4 * TT * H:64 + 5 * TT * H], small[:, 64 + 3 * TT * H:64 + 4 * TT * H], ACT.Sqrt)\
             .then_inc(post_act, 1)

            def moba_exp(h):
                act.wait_ge(bmax_ready, 2 * h + 2)
                if h >= 2:
                    act.wait_ge(pnT_ps, h - 1)
                for tt, (lo, hi) in enumerate(((0, P), (P, TRI))):
                    a.activation(smat[:, h % 2, lo:hi], expo[:, h % 2, lo:hi], ACT.Exp, bias=negmax[:, h % 2, tt:tt + 1],
                                 accum_out=psum_[:, h % 2, tt:tt + 1]).then_inc(prob_ready, 1)

            moba_exp(0)
            moba_exp(1)
            for h in range(H):
                act.wait_ge(pnT_ps, h + 1)
                if h >= 2:
                    act.wait_ge(bo_ps, h - 1)
                a.copy(dmat[:, h % 2, :], aux[:, 0, 0:TRI]).then_inc(pnT_ready, 1)
                if h + 2 < H:
                    moba_exp(h + 2)
                if h % 2:
                    act.wait_ge(bo_ps, h + 1)
                    a.copy(mixT[:, 4 + h // 2, :], aux[:, 1, 0:S]).then_inc(bo_ready, 1)

            act.wait_ge(x2_ready, 4)
            squares(1)
            for j in (0, 1):
                act.wait_ge(h2T_ps, j + 1)
                a.copy(hT[:, 2 * j:2 * j + 2, :].rearrange("p k s -> p (k s)"), hu[:, 2 + j, :]).then_inc(h2T_ready, 1)
            act.wait_ge(route, ROUTE_MASK + 1)
            for tt in range(TT):
                a.activation(gates[:, tt, :], lg[:, tt, :], ACT.Exp, bias=stat[:, 32 + tt:33 + tt]).then_inc(route_exp, 1)
            act.wait_ge(gT_ps, 1)
            a.copy(gT, po[0:E, 0, 0:S]).then_inc(gT_ready, 1)

            def gathered(count):
                act.wait_ge(xg_ps, count)
                for c in range(2):
                    a.copy(xg[:, 4 * c:4 * c + 4, :].rearrange("p k s -> p (k s)"), aux[:, c, :]).then_inc(xg_ready, 1)

            gathered(1)
            act.wait_ge(npass_ready, 1)
            npass = act.value_load(npass_i[0:1, 0:1], min_val=1, max_val=S // SLOTS)
            with act.Fori(0, npass) as ps:
                with act.Fori(0, PAIRS) as pair:
                    it = ps * PAIRS + pair
                    act.wait_ge(ghotT_ps, it + 1)
                    a.copy(ghotT, aux[:, 0, 0:S]).then_inc(ghotT_ready, 1)
                    for c in range(2):
                        act.wait_ge(glu_ready, it * 2 + (c + 1))
                        a.activation(sig[:, c * NB:(c + 1) * NB], glu[:, c * NB:(c + 1) * NB], ACT.Sigmoid,
                                     scale=ALPHA).then_inc(sig_ready, 1)
                    gathered(it + 2)
                    for c in range(2):
                        act.wait_ge(actT_ps, it * 2 + (c + 1))
                        a.copy(actT[:, 4 * c:4 * c + 4, :].rearrange("p k s -> p (k s)"), aux[:, c, :])\
                         .then_inc(actT_ready, 1)
                    act.wait_ge(chunk_done, it * PER_PAIR + (MOE0 + PER_PAIR))
                    for n in range(HALVES):
                        a.copy(out_s[:, n * NB:(n + 1) * NB], po[:, n, :]).then_inc(out_s_ready, 1)

            act.wait_ge(y_done, npass * (PAIRS * 4) + 4)
            squares(2)
            hT_lower(K // 2, 1)
            for i in range(TT * HALVES):
                tt, b = divmod(i, HALVES)
                act.wait_ge(fin_ps, i + 1)
                a.activation(lin2[:, tt, b * NB:(b + 1) * NB], hu[:, i, :], ACT.Sigmoid).then_inc(fin_sig, 1)


_INS = ['x', 'p', 'mix_norm_g', 'w_in', 'conv_w', 'conv_b', 'igate_b', 'fgate_b', 'mlstm_head_g', 'q_norm_g',
        'k_norm_g', 'w_out', 'ffn_norm_g', 'w_router', 'b_router', 'w_gate_up', 'b_gate_up', 'w_down', 'b_down',
        'ple_norm_g', 'w_ple_gate', 'w_ple_proj']


def kernel(**inputs):
    import numpy as np
    import concourse.bacc as bacc
    from concourse.bass_utils import run_bass_kernel_spmd

    nc = bacc.Bacc("TRN2", target_bir_lowering=False, num_devices=1)
    arrays, args = {}, []
    for name in _INS:
        a = np.ascontiguousarray(inputs[name])
        arrays[f"in_{name}"] = a
        args.append(nc.dram_tensor(f"in_{name}", a.shape, mybir.dt.from_np(a.dtype), kind="ExternalInput").ap())
    args.append(nc.dram_tensor("out_x", inputs["x"].shape, F32, kind="ExternalOutput").ap())
    hybrid_layer(nc, *args)
    r = run_bass_kernel_spmd(nc, [arrays], core_ids=[0])
    return r.results[0]["out_x"]
```

```python
from contextlib import ExitStack

import concourse.bass as bass
from concourse import mybir

F32 = mybir.dt.float32
I32 = mybir.dt.int32
U32 = mybir.dt.uint32
ALU = mybir.AluOpType
ACT = mybir.ActivationFunctionType
AX = mybir.AxisListType

P = 128
EPS = 1e-6
LIMIT = 7.0
ALPHA = 1.702
TOP_K = 4
MASKED = -1.0e30
RING = 6
SLOTS = 64


def hybrid_layer(nc, x, p, mix_norm_g, w_in, conv_w, conv_b, igate_b, fgate_b, mlstm_head_g, q_norm_g,
                 k_norm_g, w_out, ffn_norm_g, w_router, b_router, w_gate_up, b_gate_up, w_down, b_down,
                 ple_norm_g, w_ple_gate, w_ple_proj, out):
    S, D = x.shape[1:]
    H, DH = mlstm_head_g.shape[1:]
    E = w_router.shape[2]
    PLE = p.shape[3]
    K = D // P
    TT = S // P
    W = H * DH
    CONV = conv_w.shape[1]
    PAIRS = E // 2
    NB = 512
    HALVES = D // NB
    IG = 4 * W
    MB = IG + 2 * H
    SECTIONS = [MB, MB + W, MB + 2 * W, 0, W, 2 * W, 3 * W]
    CHUNK_QK, CHUNK_WO_B, CHUNK_PLE, CHUNK_WO_A = 3, 7, 8, 9
    J_NORM, J_VB, J_QK, J_V, J_O, J_WO_B, J_PLE, J_WO_A = 0, 4, 6, 14, 16, 18, 22, 26
    JOB_CHUNK = [0, 0, 1, 1, 2, 2, 3, 3, 3, 3, 4, 4, 4, 4, 5, 5, 6, 6] + [7] * 4 + [8] * 4 + [9] * 8
    JOBS = len(JOB_CHUNK)
    MOE0 = 10
    LATE = 16 * 10
    GATE_STEPS = 10
    POST = 7
    CONSTS = 16
    PER_PAIR = K + K // 2
    TRI = P + S
    ROWS = 10
    QUADS = TT * HALVES
    assert S == 2 * P and D == 2 * NB and W == NB and 2 * DH == P and PLE == 2 * P and E == 32
    assert PER_PAIR == 2 * RING

    ctx = ExitStack()
    with ctx:
        def sb(name, shape, dt=F32):
            return ctx.enter_context(nc.sbuf_tensor(name, shape, dt))

        def sem(name):
            return ctx.enter_context(nc.semaphore(name))

        hu = ctx.enter_context(nc.psum_tensor("hu", [P, 4, NB], F32))
        po = ctx.enter_context(nc.psum_tensor("po", [P, 2, NB], F32))
        aux = ctx.enter_context(nc.psum_tensor("aux", [P, 2, NB], F32))

        ring = sb("ring", [P, RING, 4096])
        ident = sb("ident", [P, P])
        tri = sb("tri", [P, P])
        before = sb("before", [P, P])
        ones = sb("ones", [P, P])
        dist = sb("dist", [P, TRI])
        sel_head = sb("sel_head", [H, H, P])
        iota_e = sb("iota_e", [P, E])
        iota_s = sb("iota_s", [P, SLOTS])
        cols = sb("cols", [P, K, ROWS])
        g_ffn = sb("g_ffn", [P, D])
        g_head = sb("g_head", [P, W])
        brb = sb("brb", [P, E])
        ig_bias = sb("ig_bias", [H, 1])
        fg_bias = sb("fg_bias", [H, 1])
        sel_gate = sb("sel_gate", [P, 2 * H])
        eps_t = sb("eps_t", [P, 1])
        w_r = sb("w_r", [P, K, E])
        bias = sb("bias", [P, 2, NB])
        xt = sb("xt", [P, TT, D])
        hT = sb("hT", [P, K, S])
        mixT = sb("mixT", [P, K, S])
        big1 = sb("big1", [P, TT * D])
        big2 = sb("big2", [P, K * S])
        big3 = sb("big3", [P, K * S])
        pt_in = sb("pt_in", [P, TT, PLE])
        pple = sb("pple", [P, TT, D])
        attn = sb("attn", [P, 2 * TT * H * (DH + 1) + 2 * TT * W])
        arow = sb("arow", [H, S])
        mrow = sb("mrow", [H, S])
        negm = sb("negm", [H, S])
        negmt = sb("negmt", [H, S])
        zrow = sb("zrow", [H, S])
        acol = sb("acol", [P, TT, H])
        emc = sb("emc", [P, TT, H])
        expo = sb("expo", [P, 2, TRI])
        dmat = sb("dmat", [P, 2, TRI])
        smat = sb("smat", [P, 2, TRI])
        stat = sb("stat", [P, 64])
        small = sb("small", [P, 256])
        negmax = sb("negmax", [P, 2, 2])
        psum_ = sb("psum_", [P, 2, 2])
        lg = sb("lg", [P, TT, E])
        top = sb("top", [P, TT, 8])
        topi = sb("topi", [P, TT, 8], U32)
        topf = sb("topf", [P, TT, 8])
        mask = sb("mask", [P, TT, E])
        gates = sb("gates", [P, TT, E])
        posm = sb("posm", [P, TT, E + 2])
        cnt = sb("cnt", [P, 8])
        npass_i = sb("npass_i", [1, 1], I32)

        VX = TT * H * (DH + 1)
        vx = attn[:, 0:VX].rearrange("p (t h d) -> p t h d", t=TT, h=H)
        num = attn[:, VX:2 * VX].rearrange("p (t h d) -> p t h d", t=TT, h=H)
        vb = attn[:, 2 * VX:2 * VX + TT * W].rearrange("p (t n) -> p t n", t=TT)
        og = attn[:, 2 * VX + TT * W:2 * VX + 2 * TT * W].rearrange("p (t n) -> p t n", t=TT)
        sel_expert = attn[:, 0:E * SLOTS].rearrange("p (e s) -> p e s", e=E)
        xg = attn[:, 2 * VX:2 * VX + K * P].rearrange("p (k s) -> p k s", k=K)
        w_if = attn[:, 2 * VX:2 * VX + K * 32].rearrange("p (k c) -> p k c", k=K)
        gpart = attn[:, VX:VX + S]
        rows = big3[0:ROWS, 0:D]
        fpre, fneg, fln, blog = (big3[0:H, D + i * S:D + (i + 1) * S] for i in range(4))
        pT = big2[:, 0:PLE // P * S].rearrange("p (k s) -> p k s", s=S)
        eq = big2[:, 3 * S:4 * S].rearrange("p (t e k) -> p t e k", t=TT, e=E)
        sel = dmat[:, 0, 0:P]
        onehot, ghot = (expo[:].rearrange("p a b -> p (a b)")[:, i * S:(i + 1) * S]
                        .rearrange("p (t e s) -> p t e s", t=TT, e=2) for i in range(2))
        ghotT = expo[:].rearrange("p a b -> p (a b)")[:, 2 * S:3 * S]
        xs = big1[:].rearrange("p (t d) -> p t d", t=TT)
        h2 = xs
        qkT = big2[:].rearrange("p (k s) -> p k s", k=K)
        bqT = big3[:].rearrange("p (k s) -> p k s", k=K)
        hm = xs
        normed = mixT[:].rearrange("p k s -> p (k s)").rearrange("p (i n) -> p i n", n=NB)
        glu = qkT[:].rearrange("p k s -> p (k s)")[:, 0:D]
        lin = qkT[:].rearrange("p k s -> p (k s)")[:, D:2 * D]
        sig = bqT[:].rearrange("p k s -> p (k s)")[:, 0:D]
        act_s = bqT[:].rearrange("p k s -> p (k s)")[:, D:2 * D]
        lin2 = big2[:].rearrange("p (t d) -> p t d", t=TT)
        junk = big3[:].rearrange("p (t d) -> p t d", t=TT)
        actT = mixT[:].rearrange("p k s -> p (k s)")[:, 0:D].rearrange("p (k s) -> p k s", k=K)
        out_s = mixT[:].rearrange("p k s -> p (k s)")[:, D:2 * D]

        const_ready = sem("const_ready")
        zero_ready = sem("zero_ready")
        x_loaded = [sem(f"x_loaded{t}") for t in range(TT)]
        wr_loaded = sem("wr_loaded")
        rows_loaded = sem("rows_loaded")
        small_loaded = sem("small_loaded")
        late_loaded = sem("late_loaded")
        sel_built = sem("sel_built")
        ring_full = [sem(f"ring_full{i}") for i in range(RING)]
        chunk_done = sem("chunk_done")
        job_ps = sem("job_ps")
        gpart_ps = sem("gpart_ps")
        gpart_ready = sem("gpart_ready")
        ss_ready = sem("ss_ready")
        sum_ready = sem("sum_ready")
        root_ready = sem("root_ready")
        rstd_ready = sem("rstd_ready")
        post_act = sem("post_act")
        post_sq = sem("post_sq")
        xq_ps = sem("xq_ps")
        xq_ready = sem("xq_ready")
        wr_ready = sem("wr_ready")
        logit_ps = sem("logit_ps")
        route = sem("route")
        mask_ready = sem("mask_ready")
        negtop_ready = sem("negtop_ready")
        gates_ready = sem("gates_ready")
        pos_ps = sem("pos_ps")
        cols_ps = sem("cols_ps")
        cols_ready = sem("cols_ready")
        xs_ready = sem("xs_ready")
        xT_ps = sem("xT_ps")
        hT_act = sem("hT_act")
        hT_dve = sem("hT_dve")
        gate_ps = sem("gate_ps")
        gate_step = sem("gate_step")
        gate_act = sem("gate_act")
        gcol_ps = sem("gcol_ps")
        acol_ready = sem("acol_ready")
        emc_ready = sem("emc_ready")
        conv_step = sem("conv_step")
        qk_ready = sem("qk_ready")
        v_ready = sem("v_ready")
        sq_ready = sem("sq_ready")
        nstat = sem("nstat")
        nroot = sem("nroot")
        normed_ready = sem("normed_ready")
        normT_ps = sem("normT_ps")
        bqT_ready = sem("bqT_ready")
        vb_ready = sem("vb_ready")
        og_ready = sem("og_ready")
        ogg_ready = sem("ogg_ready")
        mscore_ps = sem("mscore_ps")
        expo_ready = sem("expo_ready")
        dmat_ready = sem("dmat_ready")
        dmask_ready = sem("dmask_ready")
        smat_ready = sem("smat_ready")
        num_ps = sem("num_ps")
        num_ready = sem("num_ready")
        post_step = sem("post_step")
        hm_ready = sem("hm_ready")
        hmT_ps = sem("hmT_ps")
        hmT_ready = sem("hmT_ready")
        bscore_ps = sem("bscore_ps")
        bias_ready = sem("bias_ready")
        bmax_ready = sem("bmax_ready")
        prob_ready = sem("prob_ready")
        binv_ready = sem("binv_ready")
        pn_ready = sem("pn_ready")
        pnT_ps = sem("pnT_ps")
        pnT_ready = sem("pnT_ready")
        bo_ps = sem("bo_ps")
        bo_ready = sem("bo_ready")
        pT_ps = sem("pT_ps")
        pT_ready = sem("pT_ready")
        pple_ready = sem("pple_ready")
        x2_ready = sem("x2_ready")
        route_exp = sem("route_exp")
        npass_ready = sem("npass_ready")
        posm_step = sem("posm_step")
        y_done = sem("y_done")
        sel_ready = sem("sel_ready")
        onehot_ready = sem("onehot_ready")
        ghot_ready = sem("ghot_ready")
        ghotT_ps = sem("ghotT_ps")
        ghotT_ready = sem("ghotT_ready")
        xg_ps = sem("xg_ps")
        xg_ready = sem("xg_ready")
        glu_ready = sem("glu_ready")
        lin_ready = sem("lin_ready")
        sig_ready = sem("sig_ready")
        gated_ready = sem("gated_ready")
        act_ready = sem("act_ready")
        actT_ps = sem("actT_ps")
        actT_ready = sem("actT_ready")
        out_s_ready = sem("out_s_ready")
        scatter_ps = sem("scatter_ps")
        fin_ps = sem("fin_ps")
        fin_sig = sem("fin_sig")
        fin_step = sem("fin_step")
        stored = sem("stored")

        w_in_k = w_in[0].rearrange("(k p) n -> p k n", p=P)
        w_out_k = w_out[0].rearrange("(k p) n -> p k n", p=P)
        w_pg_k = w_ple_gate[0].rearrange("(k p) n -> p k n", p=P)
        w_pp_k = w_ple_proj[0].rearrange("(k p) n -> p k n", p=P)
        gu_src = w_gate_up[0].rearrange("e (k p) n -> k p e n", p=P)
        dn_src = w_down[0].rearrange("e (j p f) n -> j p e (f n)", p=P, f=2)
        x_src = x[0].rearrange("(t p) d -> p t d", p=P)
        p_src = p[0, 0].rearrange("(t p) d -> p t d", p=P)
        out_dst = out[0].rearrange("(t p) d -> p t d", p=P)

        def slot(n, width, parts):
            return ring[:, n % RING, 0:parts * width].rearrange("p (k n) -> p k n", n=width)

        def wait_chunk(eng, n):
            eng.wait_ge(ring_full[n % RING], 16 * (n // RING + 1))

        def last_of_chunk(j):
            return j + 1 == JOBS or JOB_CHUNK[j + 1] != JOB_CHUNK[j]

        def done_job(j, ins):
            ins.then_inc(chunk_done if last_of_chunk(j) else job_ps, 1)

        def wait_job(eng, j):
            if last_of_chunk(j):
                eng.wait_ge(chunk_done, JOB_CHUNK[j] + 1)
            else:
                eng.wait_ge(job_ps, sum(not last_of_chunk(i) for i in range(j + 1)))

        QUAD_BANKS = [hu[:, 2, :], hu[:, 3, :], po[:, 0, :], po[:, 1, :]]

        def quad(buf, q):
            return buf[:, q // HALVES, (q % HALVES) * NB:(q % HALVES + 1) * NB]

        block = ctx.enter_context(nc.Block())

        @block.sync
        def _(sp):
            for tt in range(TT):
                sp.dma_start(xt[:, tt, :], x_src[:, tt, :]).then_inc(x_loaded[tt], 16)

            def load(n, dst, src):
                if n >= RING:
                    sp.wait_ge(chunk_done, n - RING + 1)
                sp.dma_start(dst, src).then_inc(ring_full[n % RING], 16)

            sp.wait_ge(zero_ready, 1)
            sp.dma_start(rows[0:1, :], mix_norm_g).then_inc(rows_loaded, 16)
            sp.dma_start(rows[1:2, :], ple_norm_g).then_inc(rows_loaded, 16)
            sp.dma_start(rows[2:2 + CONV, :], conv_w[0]).then_inc(rows_loaded, 16)
            sp.dma_start(rows[6:7, :], conv_b).then_inc(rows_loaded, 16)
            for r, g in ((7, q_norm_g), (8, k_norm_g)):
                for c in range(2):
                    sp.dma_start(rows[r:r + 1, c * DH:(c + 1) * DH], g).then_inc(rows_loaded, 16)
            sp.dma_start(rows[9:10, :], ffn_norm_g).then_inc(rows_loaded, 16)
            load(0, slot(0, NB, K), w_in_k[:, :, SECTIONS[0]:SECTIONS[0] + NB])
            sp.wait_ge(zero_ready, 2)
            sp.dma_start(w_if[:, :, 0:2 * H], w_in_k[:, :, IG:IG + 2 * H]).then_inc(small_loaded, 16)
            sp.dma_start(ig_bias[:], igate_b.rearrange("o h -> h o")).then_inc(small_loaded, 16)
            sp.dma_start(fg_bias[:], fgate_b.rearrange("o h -> h o")).then_inc(small_loaded, 16)
            for n in range(1, len(SECTIONS)):
                load(n, slot(n, NB, K), w_in_k[:, :, SECTIONS[n]:SECTIONS[n] + NB])
                if n == 5:
                    sp.dma_start(pt_in[:], p_src).then_inc(late_loaded, 16)
                    sp.dma_start(g_head[:], mlstm_head_g[0].rearrange("h d -> (h d)")
                                 .rearrange("(o n) -> o n", o=1).to_broadcast([P, W])).then_inc(late_loaded, 16)
                    sp.dma_start(g_ffn[:], ffn_norm_g.to_broadcast([P, D])).then_inc(late_loaded, 16)
                    sp.dma_start(brb[:], b_router.to_broadcast([P, E])).then_inc(late_loaded, 16)
            load(CHUNK_WO_B, slot(CHUNK_WO_B, D, 4), w_out_k[:, 4:8, :])
            sp.dma_start(w_r[:], w_router[0].rearrange("(k p) e -> p k e", p=P)).then_inc(wr_loaded, 16)
            for j in range(4):
                sp.dma_start(bias[32 * j:32 * j + E, 0, :], b_gate_up[0][:, j * NB:(j + 1) * NB]).then_inc(late_loaded, 16)
            for j in range(HALVES):
                sp.dma_start(bias[32 * j:32 * j + E, 1, :], b_down[0][:, j * NB:(j + 1) * NB]).then_inc(late_loaded, 16)
            load(CHUNK_PLE, slot(CHUNK_PLE, D, PLE // P), w_pp_k)
            load(CHUNK_WO_A, slot(CHUNK_WO_A, D, 4), w_out_k[:, 0:4, :])

            def load_pair(it, pair):
                for c in range(PER_PAIR):
                    s = (MOE0 + c) % RING
                    sp.wait_ge(chunk_done, it * PER_PAIR + (MOE0 + c - RING + 1))
                    if c < K:
                        sp.dma_start(ring[:, s, :].rearrange("p (e n) -> p e n", e=2),
                                     gu_src[c, :, bass.ds(pair * 2, 2), :]).then_inc(ring_full[s], 16)
                    else:
                        j = c - K
                        sp.dma_start(ring[:, s, :].rearrange("p (e n) -> p e n", e=2),
                                     dn_src[j, :, bass.ds(pair * 2, 2), :]).then_inc(ring_full[s], 16)

            with sp.Fori(0, PAIRS) as pair:
                load_pair(pair, pair)
            sp.wait_ge(npass_ready, 1)
            npass = sp.value_load(npass_i[0:1, 0:1], min_val=1, max_val=S // SLOTS)
            with sp.If(npass > 1):
                with sp.Fori(1, npass) as ps:
                    with sp.Fori(0, PAIRS) as pair:
                        load_pair(ps * PAIRS + pair, pair)
            for c in range(2):
                s = (MOE0 + c) % RING
                sp.wait_ge(chunk_done, npass * (PER_PAIR * PAIRS) + (MOE0 + c - RING + 1))
                sp.dma_start(slot(MOE0 + c, D, 4), w_pg_k[:, 4 * c:4 * c + 4, :]).then_inc(ring_full[s], 16)
            for q in range(QUADS):
                sp.wait_ge(fin_step, 2 * q + 2)
                sp.dma_start(quad(out_dst, q), quad(xs, q)).then_inc(stored, 16)
            sp.wait_ge(stored, 16 * TT * HALVES)

        @block.gpsimd
        def _(pool):
            g = nc.gpsimd
            g.memset(rows, 0.0).then_inc(zero_ready, 1)
            g.memset(w_if, 0.0).then_inc(zero_ready, 1)
            g.memset(ident[:], 0.0).then_inc(zero_ready, 1)
            g.memset(sel_gate[:], 0.0).then_inc(zero_ready, 1)
            pool.wait_ge(zero_ready, 4)
            g.affine_select(out=ident[:], in_=ident[:], compare_op=ALU.not_equal, fill=1.0, base=0,
                            pattern=[[-1, P]], channel_multiplier=1).then_inc(const_ready, 1)
            g.memset(eps_t[:], EPS).then_inc(const_ready, 1)
            pool.wait_ge(const_ready, 2)
            for j in range(4):
                d = sel_gate[32 * j:32 * j + 32, :]
                g.affine_select(out=d, in_=d, compare_op=ALU.not_equal, fill=1.0, base=0,
                                pattern=[[-1, 2 * H]], channel_multiplier=1).then_inc(const_ready, 1)
            pool.wait_ge(const_ready, 6)
            g.memset(zrow[:], 0.0).then_inc(const_ready, 1)
            g.memset(tri[:], 1.0).then_inc(zero_ready, 1)
            g.memset(before[:], 1.0).then_inc(zero_ready, 1)
            g.memset(sel_head[:], 0.0).then_inc(zero_ready, 1)
            g.iota(dist[:, 0:P], pattern=[[1, P]], base=0, channel_multiplier=-1,
                   allow_small_or_imprecise_dtypes=True).then_inc(zero_ready, 1)
            g.iota(dist[:, P:TRI], pattern=[[1, S]], base=-P, channel_multiplier=-1,
                   allow_small_or_imprecise_dtypes=True).then_inc(zero_ready, 1)
            pool.wait_ge(zero_ready, 9)
            g.affine_select(out=dist[:, 0:P], in_=dist[:, 0:P], compare_op=ALU.is_ge, fill=MASKED, base=0,
                            pattern=[[-1, P]], channel_multiplier=1).then_inc(const_ready, 1)
            g.affine_select(out=dist[:, P:TRI], in_=dist[:, P:TRI], compare_op=ALU.is_ge, fill=MASKED, base=P,
                            pattern=[[-1, S]], channel_multiplier=1).then_inc(const_ready, 1)
            g.affine_select(out=tri[:], in_=tri[:], compare_op=ALU.is_ge, fill=0.0, base=0,
                            pattern=[[1, P]], channel_multiplier=-1).then_inc(const_ready, 1)
            g.affine_select(out=before[:], in_=before[:], compare_op=ALU.is_gt, fill=0.0, base=0,
                            pattern=[[1, P]], channel_multiplier=-1).then_inc(const_ready, 1)
            g.memset(ones[:], 1.0).then_inc(const_ready, 1)
            g.affine_select(out=sel_head[:], in_=sel_head[:], compare_op=ALU.not_equal, fill=1.0, base=0,
                            pattern=[[-1, H], [0, P]], channel_multiplier=1).then_inc(const_ready, 1)
            g.memset(vx[:, :, :, DH:DH + 1], 1.0).then_inc(const_ready, 1)
            g.iota(iota_e[:], pattern=[[1, E]], base=0, channel_multiplier=0,
                   allow_small_or_imprecise_dtypes=True).then_inc(const_ready, 1)
            g.iota(iota_s[:], pattern=[[1, SLOTS]], base=1, channel_multiplier=0,
                   allow_small_or_imprecise_dtypes=True).then_inc(const_ready, 1)
            def mask_decay(h):
                pool.wait_ge(dmat_ready, h + 1)
                d = dmat[:, h % 2, :].rearrange("p (b s) -> p b s", b=3)[:, 0:3:2, :]
                g.tensor_tensor(d, d, tri[:].rearrange("p (o s) -> p o s", o=1).to_broadcast([P, 2, P]),
                                ALU.mult).then_inc(dmask_ready, 1)

            def head_squares(grp):
                pool.wait_ge(post_step, POST * grp + 4)
                c = grp * S
                g.tensor_tensor(hm[:, :, W + c:W + c + S], hm[:, :, c:c + S], hm[:, :, c:c + S], ALU.mult)\
                 .then_inc(post_sq, 1)

            for h in range(4):
                mask_decay(h)
            pool.wait_ge(late_loaded, LATE)
            for tt in range(TT):
                pool.wait_ge(og_ready, tt + 1)
                g.tensor_tensor(og[:, tt, :], og[:, tt, :], g_head[:], ALU.mult).then_inc(ogg_ready, 1)
            for h in range(4, 7):
                mask_decay(h)
            head_squares(0)
            mask_decay(7)
            head_squares(1)
            pool.wait_ge(wr_loaded, 16)
            pool.wait_ge(cols_ready, 1)
            g.tensor_tensor(w_r[:], w_r[:], cols[:, :, 9:10].to_broadcast([P, K, E]), ALU.mult).then_inc(wr_ready, 1)
            pool.wait_ge(x2_ready, 12)
            g.memset(ghotT, 0.0).then_inc(ghotT_ready, 1)
            g.memset(out_s, 0.0).then_inc(out_s_ready, HALVES)
            g.memset(sel_expert[:], 0.0).then_inc(zero_ready, 1)
            pool.wait_ge(zero_ready, 10)
            for j in range(4):
                v = sel_expert[32 * j:32 * j + 32]
                g.affine_select(out=v, in_=v, compare_op=ALU.not_equal, fill=1.0, base=0,
                                pattern=[[-1, E], [0, SLOTS]], channel_multiplier=1).then_inc(sel_built, 1)

        @block.tensor
        def _(pe):
            mm = nc.tensor.matmul
            tr = nc.tensor.transpose

            def evacuated(j):
                if j < J_VB:
                    pe.wait_ge(normed_ready, j - J_NORM + 1)
                elif j < J_QK:
                    pe.wait_ge(vb_ready, j - J_VB + 1)
                elif j < J_V:
                    pe.wait_ge(conv_step, CONV * (j - J_QK + 1))
                elif j < J_O:
                    pe.wait_ge(v_ready, j - J_V + 1)
                elif j < J_WO_B:
                    pe.wait_ge(og_ready, j - J_O + 1)
                elif j < J_PLE:
                    pe.wait_ge(x2_ready, j - J_WO_B + 1)
                elif j < J_WO_A:
                    pe.wait_ge(pple_ready, j - J_PLE + 1)
                else:
                    pe.wait_ge(x2_ready, QUADS + j - J_WO_A + 1)

            def job(j):
                n = JOB_CHUNK[j]
                bank = hu[:, j % 2, :]
                if j >= 2:
                    evacuated(j - 2)
                if j == 0 or JOB_CHUNK[j - 1] != n:
                    wait_chunk(pe, n)
                if j < J_QK or J_V <= j < J_WO_B:
                    tt = j % 2
                    for k in range(K):
                        last = mm(bank, hT[:, k, tt * P:(tt + 1) * P], slot(n, NB, K)[:, k, :],
                                  start=(k == 0), stop=(k == K - 1))
                elif j < J_V:
                    ct = (j - J_QK) % 4
                    for k in range(K):
                        last = mm(bank[:, 0:S], slot(n, NB, K)[:, k, ct * P:(ct + 1) * P], hT[:, k, :],
                                  start=(k == 0), stop=(k == K - 1))
                elif J_PLE <= j < J_WO_A:
                    tt, b = divmod(j - J_PLE, HALVES)
                    for k in range(PLE // P):
                        last = mm(bank, pT[:, k, tt * P:(tt + 1) * P], slot(n, D, 2)[:, k, b * NB:(b + 1) * NB],
                                  start=(k == 0), stop=(k == 1))
                else:
                    if j < J_PLE:
                        q, ks, k0 = j - J_WO_B, range(4), 4
                    else:
                        q, ks, k0 = (j - J_WO_A) % QUADS, range(2 * ((j - J_WO_A) // QUADS), 2 * ((j - J_WO_A) // QUADS) + 2), 0
                    tt, b = divmod(q, HALVES)
                    for k in ks:
                        last = mm(bank, mixT[:, k0 + k, tt * P:(tt + 1) * P], slot(n, D, 4)[:, k, b * NB:(b + 1) * NB],
                                  start=(k == ks[0]), stop=(k == ks[-1]))
                done_job(j, last)

            pe.wait_ge(const_ready, 1)
            pe.wait_ge(rows_loaded, 16 * 9)
            for k in range(K):
                last = tr(aux[:, 0, k * ROWS:(k + 1) * ROWS], rows[:, k * P:(k + 1) * P], ident[0:ROWS, 0:ROWS])
            last.then_inc(cols_ps, 1)

            for tt in range(TT):
                pe.wait_ge(xs_ready, tt + 1)
                for k in range(K):
                    c = (k % 2) * S + tt * P
                    last = tr(QUAD_BANKS[k // 2][:, c:c + P], xs[:, tt, k * P:(k + 1) * P], ident[:])
                    if tt == 1 and k % 2:
                        last.then_inc(xT_ps, 1)

            pe.wait_ge(small_loaded, 16 * 3)
            for k in range(K):
                if k == 0:
                    pe.wait_ge(hT_act, 4)
                if k == 4:
                    pe.wait_ge(hT_dve, 4)
                c = 32 * (k % 4)
                last = mm(aux[c:c + 32, 1, 0:S], w_if[:, k, :], hT[:, k, :], start=(k < 4), stop=(k >= 4),
                          skip_group_check=True)
            last.then_inc(gpart_ps, 1)
            job(0)
            pe.wait_ge(gpart_ready, 1)
            pe.wait_ge(const_ready, 6)
            pe.wait_ge(cols_ready, 1)
            for gi in range(2):
                last = mm(aux[0:H, 0, gi * S:(gi + 1) * S], sel_gate[:, gi * H:(gi + 1) * H], gpart, start=True, stop=True)
            last.then_inc(gate_ps, 1)

            def norm_transposes(i):
                pe.wait_ge(normed_ready, i + 1)
                if i >= 2:
                    pe.wait_ge(bqT_ready, i - 1)
                elif i == 0:
                    pe.wait_ge(gate_step, GATE_STEPS)
                for j in range(4):
                    last = tr(aux[:, i % 2, j * P:(j + 1) * P], normed[:, i % 2, j * P:(j + 1) * P], ident[:])
                last.then_inc(normT_ps, 1)

            for j in range(1, 5):
                job(j)
                norm_transposes(j - 1)
                if j == 1:
                    for c, src in enumerate((arow, negmt)):
                        for tt in range(TT):
                            last = tr(hu[:, 2 + c, tt * H:(tt + 1) * H], src[:, tt * P:(tt + 1) * P], ident[0:H, 0:H])
                    last.then_inc(gcol_ps, 1)
            job(5)

            def head_rows(h):
                return slice(DH * (h % 2), DH * (h % 2) + DH)

            def moba_scores(h):
                if h == 0:
                    pe.wait_ge(bqT_ready, 4)
                if h >= 2:
                    pe.wait_ge(bias_ready, h - 1)
                r = head_rows(h)
                q, k = bqT[r, h // 2, :], bqT[r, 4 + h // 2, :]
                mm(po[:, h % 2, 0:P], q[:, 0:P], k[:, 0:P], start=True, stop=True)
                mm(po[:, h % 2, P:TRI], q[:, P:S], k, start=True, stop=True).then_inc(bscore_ps, 1)

            def moba_transposes(h):
                pe.wait_ge(pn_ready, 2 * h + 2)
                if h == 0:
                    pe.wait_ge(acol_ready, 1)
                    pe.wait_ge(emc_ready, 1)
                if h >= 2:
                    pe.wait_ge(pnT_ready, h - 1)
                for b in range(3):
                    last = tr((aux[:, 0, :] if h % 2 else hu[:, 2, :])[:, b * P:(b + 1) * P],
                              smat[:, h % 2, b * P:(b + 1) * P], ident[:])
                last.then_inc(pnT_ps, 1)

            def moba_values(h):
                pe.wait_ge(pnT_ready, h + 1)
                if h == 0:
                    pe.wait_ge(vb_ready, TT)
                if h % 2 == 0 and h >= 4:
                    pe.wait_ge(bo_ready, h // 2 - 1)
                r = head_rows(h)
                v = vb[:, :, h * DH:(h + 1) * DH]
                bank = aux[:, 1, :] if h // 2 % 2 else hu[:, 3, :]
                mm(bank[r, 0:S], v[:, 0, :], dmat[:, h % 2, 0:S], start=True, stop=False)
                mm(bank[r, P:S], v[:, 1, :], dmat[:, h % 2, S:TRI], start=False, stop=True).then_inc(bo_ps, 1)

            moba_scores(0)
            moba_scores(1)
            for h in range(H):
                job(J_QK + h)
                moba_transposes(h)
                if h >= 1:
                    moba_values(h - 1)
                if h + 2 < H:
                    moba_scores(h + 2)

            def mlstm_scores(h):
                pe.wait_ge(qk_ready, K)
                if h == 0:
                    pe.wait_ge(const_ready, CONSTS)
                    pe.wait_ge(pnT_ready, H)
                if h >= 2:
                    pe.wait_ge(smat_ready, h - 1)
                mm((aux[:, 0, :] if h % 2 else hu[:, 2, :])[:, 0:S], sel_head[:, h, :], negm[:], start=True, stop=True)
                r = head_rows(h)
                q, k = qkT[r, h // 2, :], qkT[r, 4 + h // 2, :]
                mm(po[:, h % 2, 0:S], k[:, 0:P], q, start=True, stop=True)
                mm(po[:, h % 2, S:TRI], k[:, P:S], q[:, P:S], start=True, stop=True).then_inc(mscore_ps, 1)

            def mlstm_num(h):
                pe.wait_ge(smat_ready, h + 1)
                if h == 0:
                    pe.wait_ge(v_ready, TT)
                    pe.wait_ge(bo_ready, H // 2)
                if h >= 2:
                    pe.wait_ge(num_ready, h - 1)
                s = smat[:, h % 2, :]
                n = DH + 1
                bank = aux[:, 1, :] if h % 2 else hu[:, 3, :]
                mm(bank[:, 0:n], s[:, 0:P], vx[:, 0, h, :], start=True, stop=True)
                mm(bank[:, n:2 * n], s[:, P:S], vx[:, 0, h, :], start=True, stop=False)
                mm(bank[:, n:2 * n], s[:, S:TRI], vx[:, 1, h, :], start=False, stop=True).then_inc(num_ps, 1)

            def output_transposes(grp):
                pe.wait_ge(hm_ready, grp + 1)
                bank = aux[:, 0, :] if grp else hu[:, 2, :]
                for j in range(2):
                    for tt in range(TT):
                        c = grp * S + j * P
                        last = tr(bank[:, j * S + tt * P:j * S + (tt + 1) * P], hm[:, tt, c:c + P], ident[:])
                last.then_inc(hmT_ps, 1)

            job(J_V)
            moba_values(H - 1)
            mlstm_scores(0)
            job(J_V + 1)
            mlstm_scores(1)
            for h in range(6):
                if J_O + h == J_WO_B:
                    pe.wait_ge(bo_ready, H // 2)
                job(J_O + h)
                mlstm_num(h)
                mlstm_scores(h + 2)
            pe.wait_ge(late_loaded, LATE)
            evacuated(J_PLE - 1)
            for k in range(PLE // P):
                for tt in range(TT):
                    last = tr(hu[:, 1, k * S + tt * P:k * S + tt * P + P], pt_in[:, tt, k * P:(k + 1) * P], ident[:])
            last.then_inc(pT_ps, 1)
            mlstm_num(6)
            pe.wait_ge(pT_ready, 1)
            job(J_PLE)
            mlstm_num(7)
            job(J_PLE + 1)
            output_transposes(0)
            job(J_PLE + 2)
            job(J_PLE + 3)
            pe.wait_ge(hmT_ready, 1)
            for j in range(QUADS):
                job(J_WO_A + j)
            output_transposes(1)
            pe.wait_ge(hmT_ready, 2)

            def quad_transposes(q):
                for j in range(4):
                    last = tr(QUAD_BANKS[q][:, j * P:(j + 1) * P], quad(xt, q)[:, j * P:(j + 1) * P], ident[:])
                last.then_inc(xq_ps, 1)

            def logits(tt):
                pe.wait_ge(xq_ready, HALVES * (tt + 1))
                for k in range(K):
                    last = mm(aux[:, tt, 0:E], hT[:, k, tt * P:(tt + 1) * P], w_r[:, k, :], start=(k == 0), stop=(k == K - 1))
                last.then_inc(logit_ps, 1)

            job(J_WO_A + 4)
            job(J_WO_A + 5)
            for q in range(2):
                pe.wait_ge(x2_ready, 2 * QUADS + q + 1)
                quad_transposes(q)
            job(J_WO_A + 6)
            pe.wait_ge(wr_ready, 1)
            logits(0)
            job(J_WO_A + 7)
            for q in range(2, 4):
                pe.wait_ge(x2_ready, 2 * QUADS + q + 1)
                quad_transposes(q)
            logits(1)
            pe.wait_ge(mask_ready, 1)
            mm(hu[:, 0, 0:E], before[:], mask[:, 0, :], start=True, stop=True)
            pe.wait_ge(mask_ready, 2)
            mm(hu[:, 0, E:2 * E], ones[:], mask[:, 0, :], start=True, stop=False)
            mm(hu[:, 0, E:2 * E], before[:], mask[:, 1, :], start=False, stop=True)
            mm(hu[:, 0, 2 * E:3 * E], ones[:], mask[:, 0, :], start=True, stop=False)
            mm(hu[:, 0, 2 * E:3 * E], ones[:], mask[:, 1, :], start=False, stop=True).then_inc(pos_ps, 1)

            def gather():
                for k in range(K):
                    for tt in range(TT):
                        last = mm(aux[:, k // 4, (k % 4) * P:(k % 4 + 1) * P], h2[:, tt, k * P:(k + 1) * P],
                                  onehot[:, tt, :, :].rearrange("p e s -> p (e s)"), start=(tt == 0), stop=(tt == TT - 1))
                    if k % 4 == 3:
                        last.then_inc(xg_ps, 1)

            def scatter(tt):
                for n in range(HALVES):
                    last = mm(po[:, n, :], ghotT[:, tt * P:(tt + 1) * P], out_s[:, n * NB:(n + 1) * NB],
                              start=True, stop=True)
                last.then_inc(scatter_ps, 1)

            pe.wait_ge(onehot_ready, 1)
            pe.wait_ge(xs_ready, 2 * TT)
            gather()

            pe.wait_ge(npass_ready, 1)
            npass = pe.value_load(npass_i[0:1, 0:1], min_val=1, max_val=S // SLOTS)
            with pe.Fori(0, npass) as ps:
                with pe.Fori(0, PAIRS) as pair:
                    it = ps * PAIRS + pair
                    for k in range(K):
                        if k == 0:
                            pe.wait_ge(xg_ready, it * 2 + 2)
                        if k == 1:
                            pe.wait_ge(sel_ready, it + 1)
                            for j in range(4):
                                mm(hu[:, j, :], sel[32 * j:32 * j + E, :], bias[32 * j:32 * j + E, 0, :], start=False,
                                   stop=False, skip_group_check=True)
                        if k == 2:
                            pe.wait_ge(out_s_ready, it * 2 + 2)
                            pe.wait_ge(ghotT_ready, it + 1)
                            scatter(0)
                        if k == 4:
                            pe.wait_ge(y_done, it * QUADS + 2)
                            scatter(1)
                        if k == 5:
                            pe.wait_ge(ghot_ready, it + 1)
                            for tt in range(TT):
                                last = tr(aux[:, 0, tt * P:(tt + 1) * P], ghot[:, tt, :, :].rearrange("p e s -> p (e s)"),
                                          ident[:])
                            last.then_inc(ghotT_ps, 1)
                        s = (MOE0 + k) % RING
                        pe.wait_ge(ring_full[s], it * 32 + 16 * ((MOE0 + k) // RING + 1))
                        for j in range(4):
                            for e in range(2):
                                last = mm(hu[e * SLOTS:(e + 1) * SLOTS, j, :], xg[:, k, e * SLOTS:(e + 1) * SLOTS],
                                          ring[:, s, e * 2048 + j * NB:e * 2048 + (j + 1) * NB],
                                          start=(k == 0), stop=(k == K - 1), skip_group_check=True)
                        last.then_inc(chunk_done, 1)
                    pe.wait_ge(onehot_ready, it + 2)
                    pe.wait_ge(ghotT_ready, it + 2)
                    gather()
                    for c in range(2):
                        pe.wait_ge(xg_ready, it * 2 + (3 + c))
                        pe.wait_ge(act_ready, it * 2 + (c + 1))
                        for b in range(4):
                            c0 = (2 * c + b // 2) * 2 * P + b % 2
                            last = tr(aux[:, c, b * P:(b + 1) * P], act_s[:, c0:c0 - b % 2 + 2 * P:2], ident[:])
                        last.then_inc(actT_ps, 1)
                    pe.wait_ge(y_done, it * QUADS + QUADS)
                    for n in range(HALVES):
                        mm(po[:, n, :], sel[32 * n:32 * n + E, :], bias[32 * n:32 * n + E, 1, :], start=True, stop=False,
                           skip_group_check=True)
                    for j in range(K // 2):
                        c = K + j
                        s = (MOE0 + c) % RING
                        if j % 2 == 0:
                            pe.wait_ge(actT_ready, it * 2 + (j // 2 + 1))
                        pe.wait_ge(ring_full[s], it * 32 + 16 * ((MOE0 + c) // RING + 1))
                        for f in range(2):
                            for n in range(HALVES):
                                for e in range(2):
                                    o = (e * 2 + f) * D + n * NB
                                    last = mm(po[e * SLOTS:(e + 1) * SLOTS, n, :],
                                              actT[:, 2 * j + f, e * SLOTS:(e + 1) * SLOTS], ring[:, s, o:o + NB],
                                              start=False, stop=(j == K // 2 - 1 and f == 1),
                                              skip_group_check=True)
                        last.then_inc(chunk_done, 1)

            pe.wait_ge(out_s_ready, npass * (2 * PAIRS) + 2)
            pe.wait_ge(ghotT_ready, npass * PAIRS + 1)
            for tt in range(TT):
                pe.wait_ge(y_done, npass * (PAIRS * QUADS) + 2 * tt)
                scatter(tt)
            pe.wait_ge(y_done, npass * (PAIRS * QUADS) + QUADS)

            for q in range(QUADS):
                quad_transposes(q)
            for tt in range(TT):
                pe.wait_ge(hT_act, 8 + 4 * tt)
                pe.wait_ge(hT_dve, 8 + 4 * tt)
                for n in range(HALVES):
                    for k in range(K):
                        if tt == 0 and n == 0 and k % 4 == 0:
                            c = k // 4
                            pe.wait_ge(ring_full[(MOE0 + c) % RING], npass * (PAIRS * 32) + 16 * ((MOE0 + c) // RING + 1))
                        last = mm(hu[:, (tt * 2 + n) % 2, :] if tt == 0 else aux[:, n, :], hT[:, k, tt * P:(tt + 1) * P],
                                  slot(MOE0 + k // 4, D, 4)[:, k % 4, n * NB:(n + 1) * NB],
                                  start=(k == 0), stop=(k == K - 1))
                    last.then_inc(fin_ps, 1)

        @block.vector
        def _(dve):
            v = nc.vector

            def rstd(i):
                dve.wait_ge(root_ready, i + 1)
                v.reciprocal(stat[:, 16 + i:17 + i], stat[:, 8 + i:9 + i]).then_inc(rstd_ready, 1)
                dve.wait_ge(rstd_ready, i + 1)
                return stat[:, 16 + i:17 + i]

            for tt in range(TT):
                r = rstd(tt)
                v.tensor_scalar(xs[:, tt, :], xt[:, tt, :], r, None, ALU.mult).then_inc(xs_ready, 1)
            dve.wait_ge(cols_ps, 1)
            v.tensor_copy(cols[:].rearrange("p k r -> p (k r)"), aux[:, 0, 0:K * ROWS]).then_inc(cols_ready, 1)
            dve.wait_ge(cols_ready, 1)
            for k in range(4, K):
                dve.wait_ge(xT_ps, k // 2 + 1)
                v.tensor_scalar(hT[:, k, :], QUAD_BANKS[k // 2][:, (k % 2) * S:(k % 2) * S + S],
                                cols[:, k, 0:1], None, ALU.mult).then_inc(hT_dve, 1)
            dve.wait_ge(gpart_ps, 1)
            v.tensor_copy(gpart, aux[:, 1, 0:S]).then_inc(gpart_ready, 1)

            def normed_half(i):
                ss = small[:, 0:H]
                dve.wait_ge(sq_ready, i + 1)
                v.tensor_reduce(ss, xs[:, i % 2, 0:W].rearrange("p (h d) -> p h d", h=H), AX.X, ALU.add).then_inc(nstat, 1)
                dve.wait_ge(nroot, i + 1)
                v.reciprocal(small[:, 3 * H:4 * H], small[:, 2 * H:3 * H]).then_inc(nstat, 1)
                dve.wait_ge(nstat, 2 * i + 2)
                if i >= 2:
                    dve.wait_ge(normT_ps, i - 1)
                v.tensor_tensor(normed[:, i % 2, :].rearrange("p (h d) -> p h d", h=H),
                                hu[:, i % 2, :].rearrange("p (h d) -> p h d", h=H),
                                small[:, 3 * H:4 * H].rearrange("p (h o) -> p h o", o=1).to_broadcast([P, H, DH]),
                                ALU.mult).then_inc(normed_ready, 1)

            def normed_transposed(i):
                dve.wait_ge(normT_ps, i + 1)
                j, tt = 4 * (i // 2), i % 2
                v.tensor_scalar(bqT[:, j:j + 4, tt * P:(tt + 1) * P],
                                aux[:, i % 2, :].rearrange("p (j t) -> p j t", j=4),
                                cols[:, 0, 7 + i // 2:8 + i // 2], DH ** -0.5 if i < 2 else 1.0,
                                ALU.mult, ALU.mult).then_inc(bqT_ready, 1)

            normed_half(0)
            dve.wait_ge(gate_ps, 1)
            dve.wait_ge(const_ready, 7)
            n = [0]

            def gate(ins):
                n[0] += 1
                ins.then_inc(gate_step, 1)
                dve.wait_ge(gate_step, n[0])

            gate(v.tensor_scalar(fpre, aux[0:H, 0, S:2 * S], fg_bias[:, 0:1], None, ALU.add))
            gate(v.tensor_scalar(fneg, fpre, -1.0, None, ALU.mult))
            gate(v.tensor_tensor(fneg, fneg, fpre, ALU.min))
            gate(v.tensor_scalar(fpre, fpre, 0.0, None, ALU.min))
            dve.wait_ge(gate_act, 2)
            gate(v.tensor_tensor(fpre, fpre, fln, ALU.subtract))
            gate(v.tensor_tensor_scan(blog, zrow[:], fpre, 0.0, ALU.add, ALU.add))
            gate(v.scalar_tensor_tensor(out=arow[:], in0=aux[0:H, 0, 0:S], scalar=ig_bias[:, 0:1], in1=blog,
                                        op0=ALU.add, op1=ALU.subtract))
            gate(v.tensor_tensor_scan(mrow[:], zrow[:], arow[:], 0.0, ALU.add, ALU.max))
            gate(v.tensor_scalar(negm[:], mrow[:], -1.0, None, ALU.mult))
            gate(v.scalar_tensor_tensor(out=negmt[:], in0=mrow[:], scalar=-1.0, in1=blog,
                                        op0=ALU.mult, op1=ALU.subtract))
            assert n[0] == GATE_STEPS
            for i in range(1, 4):
                normed_half(i)
                normed_transposed(i - 1)
                if i == 1:
                    dve.wait_ge(gcol_ps, 1)
                    v.tensor_copy(acol[:].rearrange("p t h -> p (t h)"), hu[:, 2, 0:TT * H]).then_inc(acol_ready, 1)
            normed_transposed(3)

            def moba_max(h):
                dve.wait_ge(bscore_ps, h + 1)
                slope = 2.0 ** (-8.0 * (h + 1) / H)
                b = expo[:, h % 2, :]
                v.scalar_tensor_tensor(out=b, in0=dist[:], scalar=slope, in1=po[:, h % 2, 0:TRI],
                                       op0=ALU.mult, op1=ALU.add).then_inc(bias_ready, 1)
                dve.wait_ge(bias_ready, h + 1)
                v.tensor_reduce(negmax[:, h % 2, 0:1], b[:, 0:P], AX.X, ALU.max, negate=True).then_inc(bmax_ready, 1)
                v.tensor_reduce(negmax[:, h % 2, 1:2], b[:, P:TRI], AX.X, ALU.max, negate=True).then_inc(bmax_ready, 1)

            dve.wait_ge(const_ready, CONSTS)
            moba_max(0)
            moba_max(1)
            for h in range(H):
                dve.wait_ge(prob_ready, 2 * h + 2)
                inv = small[:, 48 + 2 * (h % 2):50 + 2 * (h % 2)]
                v.reciprocal(inv, psum_[:, h % 2, :]).then_inc(binv_ready, 1)
                dve.wait_ge(binv_ready, h + 1)
                for tt, (lo, hi) in enumerate(((0, P), (P, TRI))):
                    v.tensor_scalar(smat[:, h % 2, lo:hi], smat[:, h % 2, lo:hi], inv[:, tt:tt + 1], None,
                                    ALU.mult).then_inc(pn_ready, 1)
                wait_job(dve, J_QK + h)
                src = hu[:, h % 2, 0:S]
                v.tensor_scalar(qkT[:, h, :], src, cols[:, h, 5:6], cols[:, h, 6:7], ALU.mult, ALU.add)\
                 .then_inc(conv_step, 1)
                for back in range(1, CONV):
                    dve.wait_ge(conv_step, CONV * h + back)
                    v.scalar_tensor_tensor(out=qkT[:, h, back:S], in0=src[:, 0:S - back],
                                           scalar=cols[:, h, 5 - back:6 - back], in1=qkT[:, h, back:S],
                                           op0=ALU.mult, op1=ALU.add).then_inc(conv_step, 1)
                if h + 2 < H:
                    moba_max(h + 2)

            def residual(j):
                wait_job(dve, j)
                i = j - J_WO_B if j < J_PLE else QUADS + j - J_WO_A
                if i >= QUADS:
                    dve.wait_ge(x2_ready, i - QUADS + 1)
                x_q = quad(xt, i % QUADS)
                v.tensor_tensor(x_q, x_q, hu[:, j % 2, :], ALU.add).then_inc(x2_ready, 1)

            post = [0]

            def step(ins):
                post[0] += 1
                ins.then_inc(post_step, 1)
                dve.wait_ge(post_step, post[0])

            def mlstm_output(grp):
                heads = slice(4 * grp, 4 * grp + 4)

                def st(c):
                    return small[:, 64 + 8 * c:72 + 8 * c].rearrange("p (t h) -> p t h", t=TT)

                def wide(c):
                    return st(c).rearrange("p t (h o) -> p t h o", o=1).to_broadcast([P, TT, 4, DH])

                dve.wait_ge(num_ready, 4 * grp + 4)
                dve.wait_ge(emc_ready, 1)
                den = num[:, :, heads, DH]
                h4 = hm[:, :, grp * S:(grp + 1) * S]
                h4 = h4.rearrange("p t (h d) -> p t h d", h=4)
                sq4 = hm[:, :, W + grp * S:W + (grp + 1) * S].rearrange("p t (h d) -> p t h d", h=4)
                step(v.scalar_tensor_tensor(out=st(0), in0=den, scalar=-1.0, in1=den, op0=ALU.mult, op1=ALU.max))
                step(v.tensor_tensor(st(0), st(0), emc[:, :, heads], ALU.max))
                step(v.reciprocal(st(1), st(0)))
                step(v.tensor_tensor(h4, num[:, :, heads, 0:DH], wide(1), ALU.mult))
                dve.wait_ge(post_sq, grp + 1)
                step(v.tensor_reduce(st(2), sq4, AX.X, ALU.add))
                dve.wait_ge(post_act, grp + 1)
                step(v.reciprocal(st(4), st(3)))
                step(v.tensor_tensor(h4, h4, wide(4), ALU.mult))
                dve.wait_ge(ogg_ready, TT)
                h3, g3 = (b[:, :, grp * S:(grp + 1) * S] for b in (hm, og))
                v.tensor_tensor(h3, h3, g3, ALU.mult).then_inc(hm_ready, 1)

            steps = [0]

            def routed(ins, wait=True):
                steps[0] += 1
                ins.then_inc(route, 1)
                if wait:
                    dve.wait_ge(route, steps[0])

            def route_tile(tt):
                dve.wait_ge(ss_ready, TT + HALVES * (tt + 1))
                c = 24 + 2 * tt
                v.tensor_tensor(stat[:, 2 + tt:3 + tt], stat[:, c:c + 1], stat[:, c + 1:c + 2], ALU.add).then_inc(sum_ready, 1)
                r = rstd(TT + tt)
                dve.wait_ge(late_loaded, LATE)
                dve.wait_ge(logit_ps, tt + 1)
                routed(v.scalar_tensor_tensor(out=lg[:, tt, :], in0=aux[:, tt, 0:E], scalar=r, in1=brb[:],
                                              op0=ALU.mult, op1=ALU.add))
                routed(v.max(top[:, tt, :], lg[:, tt, :]))
                routed(v.max_index(topi[:, tt, :], top[:, tt, :], lg[:, tt, :]))
                routed(v.tensor_copy(topf[:, tt, :], topi[:, tt, :]))
                routed(v.tensor_tensor(eq[:, tt, :, :],
                                       iota_e[:].rearrange("p (e o) -> p e o", o=1).to_broadcast([P, E, TOP_K]),
                                       topf[:, tt, 0:TOP_K].rearrange("p (o k) -> p o k", o=1).to_broadcast([P, E, TOP_K]),
                                       ALU.is_equal))
                v.tensor_reduce(mask[:, tt, :], eq[:, tt, :, :], AX.X, ALU.add).then_inc(mask_ready, 1)
                v.tensor_scalar(stat[:, 32 + tt:33 + tt], top[:, tt, 0:1], -1.0, None, ALU.mult).then_inc(negtop_ready, 1)
                v.scalar_tensor_tensor(out=xs[:, tt, :], in0=xt[:, tt, :], scalar=r, in1=g_ffn[:],
                                       op0=ALU.mult, op1=ALU.mult).then_inc(xs_ready, 1)

            for h in range(H):
                dve.wait_ge(mscore_ps, h + 1)
                b = (aux[:, 0, :] if h % 2 else hu[:, 2, :])[:, 0:S]
                v.tensor_scalar(expo[:, h % 2, 0:S], b, acol[:, 0, h:h + 1], 0.0, ALU.add, ALU.min)\
                 .then_inc(expo_ready, 1)
                v.tensor_scalar(expo[:, h % 2, S:TRI], b[:, P:S], acol[:, 1, h:h + 1], 0.0, ALU.add, ALU.min)\
                 .then_inc(expo_ready, 1)
                dve.wait_ge(dmask_ready, h + 1)
                if h >= 2:
                    dve.wait_ge(num_ps, h - 1)
                v.scalar_tensor_tensor(out=smat[:, h % 2, :], in0=po[:, h % 2, 0:TRI], scalar=DH ** -0.5,
                                       in1=dmat[:, h % 2, :], op0=ALU.mult, op1=ALU.mult).then_inc(smat_ready, 1)
                if h >= 4:
                    residual(J_WO_B + h - 4)
                if h == 6:
                    mlstm_output(0)
            mlstm_output(1)
            dve.wait_ge(wr_loaded, 16)
            for j in range(2 * QUADS):
                residual(J_WO_A + j)
                if j == QUADS + 1 or j == 2 * QUADS - 1:
                    route_tile(j // 2 % 2)

            dve.wait_ge(pos_ps, 1)
            routed(v.scalar_tensor_tensor(out=posm[:, :, 0:E], in0=hu[:, 0, 0:TT * E].rearrange("p (t e) -> p t e", t=TT),
                                          scalar=1.0, in1=mask[:], op0=ALU.add, op1=ALU.mult))
            routed(v.tensor_scalar(posm[:, :, E:E + 2], posm[:, :, 0:2], -float(SLOTS), None, ALU.add))
            routed(v.tensor_reduce(cnt[:, 0:1], hu[:, 0, 2 * E:3 * E], AX.X, ALU.max), False)

            def one_hot(first):
                v.tensor_tensor(onehot, iota_s[:].rearrange("p (a b s) -> p a b s", a=1, b=1).to_broadcast([P, TT, 2, SLOTS]),
                                posm[:, :, first].rearrange("p t (e o) -> p t e o", o=1).to_broadcast([P, TT, 2, SLOTS]),
                                ALU.is_equal).then_inc(onehot_ready, 1)

            one_hot(slice(0, 2))
            dve.wait_ge(route, steps[0])
            for j in range(1, S // SLOTS):
                routed(v.tensor_scalar(cnt[:, j:j + 1], cnt[:, 0:1], float(j * SLOTS), None, ALU.is_gt), j == 3)
            routed(v.tensor_reduce(cnt[:, 4:5], cnt[:, 1:4], AX.X, ALU.add))
            v.tensor_scalar(npass_i[:], cnt[0:1, 4:5], 1.0, None, ALU.add).then_inc(npass_ready, 1)
            dve.wait_ge(route_exp, TT)
            routed(v.tensor_tensor(gates[:], gates[:], mask[:], ALU.mult))
            routed(v.tensor_reduce(stat[:, 34:36], gates[:], AX.X, ALU.add))
            routed(v.reciprocal(stat[:, 36:38], stat[:, 34:36]))
            for tt in range(TT):
                v.tensor_scalar(gates[:, tt, :], gates[:, tt, :], stat[:, 36 + tt:37 + tt], None, ALU.mult)\
                 .then_inc(gates_ready, 1)
            dve.wait_ge(gates_ready, TT)

            def add_y(tt):
                for n in range(HALVES):
                    q = tt * HALVES + n
                    v.tensor_tensor(quad(xt, q), quad(xt, q), po[:, n, :], ALU.add).then_inc(y_done, 1)

            dve.wait_ge(sel_built, 4)
            dve.wait_ge(npass_ready, 1)
            npass = dve.value_load(npass_i[0:1, 0:1], min_val=1, max_val=S // SLOTS)
            with dve.Fori(0, npass) as ps:
                with dve.Fori(0, PAIRS) as pair:
                    it = ps * PAIRS + pair
                    dve.wait_ge(chunk_done, it * PER_PAIR + MOE0)
                    v.tensor_copy(sel.rearrange("p (e s) -> p e s", e=2), sel_expert[:, bass.ds(pair * 2, 2), :])\
                     .then_inc(sel_ready, 1)
                    dve.wait_ge(onehot_ready, it + 1)
                    gp = gates[:, :, bass.ds(pair * 2, 2)]
                    v.tensor_tensor(ghot, onehot, gp.rearrange("p t (e o) -> p t e o", o=1)
                                    .to_broadcast([P, TT, 2, SLOTS]), ALU.mult).then_inc(ghot_ready, 1)
                    dve.wait_ge(ghot_ready, it + 1)
                    dve.wait_ge(xg_ps, it * 2 + 2)
                    one_hot(bass.ds(pair * 2 + 2, 2))
                    for tt in range(TT):
                        dve.wait_ge(scatter_ps, it * TT + (tt + 1))
                        add_y(tt)
                    dve.wait_ge(y_done, it * QUADS + QUADS)
                    dve.wait_ge(chunk_done, it * PER_PAIR + (MOE0 + K))
                    for c in range(2):
                        v.tensor_scalar(glu[:, c * NB:(c + 1) * NB], hu[:, c, :], LIMIT, None, ALU.min)\
                         .then_inc(glu_ready, 1)
                    for c in range(2):
                        v.tensor_scalar(lin[:, c * NB:(c + 1) * NB], hu[:, 2 + c, :], LIMIT, -LIMIT, ALU.min, ALU.max)\
                         .then_inc(lin_ready, 1)
                    dve.wait_ge(lin_ready, it * 2 + 2)
                    for c in range(2):
                        q = slice(c * NB, (c + 1) * NB)
                        dve.wait_ge(sig_ready, it * 2 + (c + 1))
                        v.tensor_tensor(glu[:, q], glu[:, q], sig[:, q], ALU.mult).then_inc(gated_ready, 1)
                        dve.wait_ge(gated_ready, it * 2 + (c + 1))
                        v.scalar_tensor_tensor(out=act_s[:, q], in0=lin[:, q], scalar=1.0, in1=glu[:, q],
                                               op0=ALU.add, op1=ALU.mult).then_inc(act_ready, 1)
                dve.wait_ge(onehot_ready, ps * PAIRS + (PAIRS + 1))
                v.tensor_scalar(posm[:], posm[:], -float(SLOTS), None, ALU.add).then_inc(posm_step, 1)
                dve.wait_ge(posm_step, ps + 1)
            for tt in range(TT):
                dve.wait_ge(scatter_ps, npass * (PAIRS * TT) + (tt + 1))
                add_y(tt)

            def quad_columns(q):
                dve.wait_ge(xq_ps, QUADS + q + 1)
                for j in range(4):
                    k = 4 * (q % HALVES) + j
                    v.tensor_scalar(hT[:, k, q // HALVES * P:(q // HALVES + 1) * P], QUAD_BANKS[q][:, j * P:(j + 1) * P],
                                    cols[:, k, 1:2], None, ALU.mult).then_inc(hT_dve, 1)

            for tt in range(TT):
                quad_columns(2 * tt + 1)
            for tt in range(TT):
                dve.wait_ge(ss_ready, 3 * TT + HALVES * (tt + 1))
                c = 28 + 2 * tt
                v.tensor_tensor(stat[:, 4 + tt:5 + tt], stat[:, c:c + 1], stat[:, c + 1:c + 2], ALU.add).then_inc(sum_ready, 1)
                rstd(2 * TT + tt)
            for q in range(QUADS):
                dve.wait_ge(fin_sig, q + 1)
                v.tensor_tensor(quad(xs, q), quad(lin2, q), quad(pple, q), ALU.mult).then_inc(fin_step, 1)
                dve.wait_ge(fin_step, 2 * q + 1)
                v.tensor_tensor(quad(xs, q), quad(xs, q), quad(xt, q), ALU.add).then_inc(fin_step, 1)

        @block.scalar
        def _(act):
            a = nc.scalar

            def root(i, src, wait):
                if wait:
                    act.wait_ge(sum_ready, i - 1)
                a.activation(stat[:, 8 + i:9 + i], src, ACT.Sqrt, scale=1.0 / D, bias=eps_t[:]).then_inc(root_ready, 1)

            act.wait_ge(const_ready, 2)
            for tt in range(TT):
                act.wait_ge(x_loaded[tt], 16)
                a.activation(xs[:, tt, :], xt[:, tt, :], ACT.Square, accum_out=stat[:, tt:tt + 1]).then_inc(ss_ready, 1)
                act.wait_ge(ss_ready, tt + 1)
                root(tt, stat[:, tt:tt + 1], False)
            act.wait_ge(cols_ready, 1)
            for k in range(4):
                act.wait_ge(xT_ps, k // 2 + 1)
                a.activation(hT[:, k, :], QUAD_BANKS[k // 2][:, (k % 2) * S:(k % 2) * S + S], ACT.Copy,
                             scale=cols[:, k, 0:1]).then_inc(hT_act, 1)

            for i in range(4):
                wait_job(act, J_NORM + i)
                if i >= 2:
                    act.wait_ge(nstat, 2 * (i - 2) + 1)
                a.activation(xs[:, i % 2, 0:W], hu[:, i % 2, :], ACT.Square).then_inc(sq_ready, 1)
                act.wait_ge(nstat, 2 * i + 1)
                a.activation(small[:, 2 * H:3 * H], small[:, 0:H], ACT.Sqrt, scale=1.0 / DH, bias=eps_t[:]).then_inc(nroot, 1)
                if i == 0:
                    act.wait_ge(gate_step, 3)
                    a.activation(fln, fneg, ACT.Exp).then_inc(gate_act, 1)
                    act.wait_ge(gate_act, 1)
                    a.activation(fln, fln, ACT.Ln, bias=1.0).then_inc(gate_act, 1)
            act.wait_ge(gcol_ps, 1)
            a.activation(emc[:].rearrange("p t h -> p (t h)"), hu[:, 3, 0:TT * H], ACT.Exp).then_inc(emc_ready, 1)
            for tt in range(TT):
                wait_job(act, J_VB + tt)
                a.copy(vb[:, tt, :], hu[:, tt, :]).then_inc(vb_ready, 1)

            def moba_exp(h):
                act.wait_ge(bmax_ready, 2 * h + 2)
                if h >= 2:
                    act.wait_ge(pnT_ps, h - 1)
                for tt, (lo, hi) in enumerate(((0, P), (P, TRI))):
                    a.activation(smat[:, h % 2, lo:hi], expo[:, h % 2, lo:hi], ACT.Exp, bias=negmax[:, h % 2, tt:tt + 1],
                                 accum_out=psum_[:, h % 2, tt:tt + 1]).then_inc(prob_ready, 1)

            def moba_pair(i):
                act.wait_ge(bo_ps, 2 * i + 2)
                a.copy(mixT[:, 4 + i, :], (aux[:, 1, :] if i % 2 else hu[:, 3, :])[:, 0:S]).then_inc(bo_ready, 1)

            moba_exp(0)
            moba_exp(1)
            for h in range(H):
                act.wait_ge(pnT_ps, h + 1)
                if h >= 2:
                    act.wait_ge(bo_ps, h - 1)
                a.copy(dmat[:, h % 2, :], (aux[:, 0, :] if h % 2 else hu[:, 2, :])[:, 0:TRI]).then_inc(pnT_ready, 1)
                if h + 2 < H:
                    moba_exp(h + 2)
                if h % 2 == 0 and h >= 2:
                    moba_pair(h // 2 - 1)
            for i in range(K):
                act.wait_ge(conv_step, CONV * (i + 1))
                a.activation(qkT[:, i, :], qkT[:, i, :], ACT.Silu).then_inc(qk_ready, 1)
            act.wait_ge(const_ready, CONSTS)

            def v_tile(tt):
                wait_job(act, J_V + tt)
                a.copy(vx[:, tt, :, 0:DH], hu[:, tt, :].rearrange("p (h d) -> p h d", h=H)).then_inc(v_ready, 1)

            def decay(h):
                act.wait_ge(expo_ready, 2 * h + 2)
                if h == 0:
                    act.wait_ge(bo_ps, H)
                a.activation(dmat[:, h % 2, :], expo[:, h % 2, :], ACT.Exp).then_inc(dmat_ready, 1)

            def numerator(h):
                act.wait_ge(num_ps, h + 1)
                a.copy(num[:, :, h, :], (aux[:, 1, :] if h % 2 else hu[:, 3, :])[:, 0:2 * (DH + 1)]
                       .rearrange("p (t d) -> p t d", t=TT)).then_inc(num_ready, 1)

            def ple_tile(q):
                wait_job(act, J_PLE + q)
                a.copy(quad(pple, q), hu[:, (J_PLE + q) % 2, :]).then_inc(pple_ready, 1)

            def head_roots(grp):
                act.wait_ge(post_step, POST * grp + 5)
                a.activation(small[:, 88:96], small[:, 80:88], ACT.Sqrt, scale=1.0 / DH, bias=eps_t[:]).then_inc(post_act, 1)

            def output_tile(grp):
                act.wait_ge(hmT_ps, grp + 1)
                a.copy(mixT[:, 2 * grp:2 * grp + 2, :].rearrange("p k s -> p (k s)"),
                       aux[:, 0, :] if grp else hu[:, 2, :]).then_inc(hmT_ready, 1)

            v_tile(0)
            moba_pair(3)
            decay(0)
            v_tile(1)
            decay(1)
            for h in range(6):
                if h < TT:
                    wait_job(act, J_O + h)
                    a.activation(og[:, h, :], hu[:, h, :], ACT.Sigmoid).then_inc(og_ready, 1)
                numerator(h)
                decay(h + 2)
                if h == 4:
                    head_roots(0)
            act.wait_ge(pT_ps, 1)
            a.copy(pT.rearrange("p k s -> p (k s)"), hu[:, 1, :]).then_inc(pT_ready, 1)
            numerator(6)
            ple_tile(0)
            numerator(7)
            ple_tile(1)
            output_tile(0)
            head_roots(1)
            ple_tile(2)
            ple_tile(3)
            output_tile(1)

            def quad_squares(q, col):
                a.activation(quad(junk, q), quad(xt, q), ACT.Square, accum_out=stat[:, col:col + 1]).then_inc(ss_ready, 1)

            for q in range(QUADS):
                act.wait_ge(x2_ready, 2 * QUADS + q + 1)
                quad_squares(q, 24 + q)
                if q % 2 == 1:
                    root(TT + q // 2, stat[:, 2 + q // 2:3 + q // 2], True)
                act.wait_ge(xq_ps, q + 1)
                tt, n = divmod(q, HALVES)
                a.copy(hT[:, 4 * n:4 * n + 4, tt * P:(tt + 1) * P], QUAD_BANKS[q].rearrange("p (j t) -> p j t", j=4))\
                 .then_inc(xq_ready, 1)
            for tt in range(TT):
                act.wait_ge(negtop_ready, tt + 1)
                a.activation(gates[:, tt, :], lg[:, tt, :], ACT.Exp, bias=stat[:, 32 + tt:33 + tt]).then_inc(route_exp, 1)

            def gathered(count):
                for c in range(2):
                    act.wait_ge(xg_ps, count + (c + 1))
                    a.copy(xg[:, 4 * c:4 * c + 4, :].rearrange("p k s -> p (k s)"), aux[:, c, :]).then_inc(xg_ready, 1)

            gathered(0)
            act.wait_ge(npass_ready, 1)
            npass = act.value_load(npass_i[0:1, 0:1], min_val=1, max_val=S // SLOTS)
            with act.Fori(0, npass) as ps:
                with act.Fori(0, PAIRS) as pair:
                    it = ps * PAIRS + pair
                    act.wait_ge(ghotT_ps, it + 1)
                    a.copy(ghotT, aux[:, 0, 0:S]).then_inc(ghotT_ready, 1)
                    for c in range(2):
                        act.wait_ge(glu_ready, it * 2 + (c + 1))
                        a.activation(sig[:, c * NB:(c + 1) * NB], glu[:, c * NB:(c + 1) * NB], ACT.Sigmoid,
                                     scale=ALPHA).then_inc(sig_ready, 1)
                    gathered(it * 2 + 2)
                    for c in range(2):
                        act.wait_ge(actT_ps, it * 2 + (c + 1))
                        a.copy(actT[:, 4 * c:4 * c + 4, :].rearrange("p k s -> p (k s)"), aux[:, c, :])\
                         .then_inc(actT_ready, 1)
                    act.wait_ge(chunk_done, it * PER_PAIR + (MOE0 + PER_PAIR))
                    for n in range(HALVES):
                        a.copy(out_s[:, n * NB:(n + 1) * NB], po[:, n, :]).then_inc(out_s_ready, 1)

            for q in range(QUADS):
                act.wait_ge(y_done, npass * (PAIRS * QUADS) + (q + 1))
                quad_squares(q, 28 + q)
            for tt in range(TT):
                q = 2 * tt
                act.wait_ge(xq_ps, QUADS + q + 1)
                for j in range(4):
                    a.activation(hT[:, j, tt * P:(tt + 1) * P], QUAD_BANKS[q][:, j * P:(j + 1) * P], ACT.Copy,
                                 scale=cols[:, j, 1:2]).then_inc(hT_act, 1)
            for tt in range(TT):
                root(2 * TT + tt, stat[:, 4 + tt:5 + tt], True)
            for q in range(QUADS):
                tt, n = divmod(q, HALVES)
                act.wait_ge(rstd_ready, 2 * TT + tt + 1)
                act.wait_ge(fin_ps, q + 1)
                a.activation(quad(lin2, q), hu[:, n, :] if tt == 0 else aux[:, n, :], ACT.Sigmoid,
                             scale=stat[:, 16 + 2 * TT + tt:17 + 2 * TT + tt]).then_inc(fin_sig, 1)


_INS = ['x', 'p', 'mix_norm_g', 'w_in', 'conv_w', 'conv_b', 'igate_b', 'fgate_b', 'mlstm_head_g', 'q_norm_g',
        'k_norm_g', 'w_out', 'ffn_norm_g', 'w_router', 'b_router', 'w_gate_up', 'b_gate_up', 'w_down', 'b_down',
        'ple_norm_g', 'w_ple_gate', 'w_ple_proj']


def kernel(**inputs):
    import numpy as np
    import concourse.bacc as bacc
    from concourse.bass_utils import run_bass_kernel_spmd

    nc = bacc.Bacc("TRN2", target_bir_lowering=False, num_devices=1)
    arrays, args = {}, []
    for name in _INS:
        a = np.ascontiguousarray(inputs[name])
        arrays[f"in_{name}"] = a
        args.append(nc.dram_tensor(f"in_{name}", a.shape, mybir.dt.from_np(a.dtype), kind="ExternalInput").ap())
    args.append(nc.dram_tensor("out_x", inputs["x"].shape, F32, kind="ExternalOutput").ap())
    hybrid_layer(nc, *args)
    r = run_bass_kernel_spmd(nc, [arrays], core_ids=[0])
    return r.results[0]["out_x"]
```
